# Optimizing a Trainium2 kernel written in Bass

```python
import jax, jax.numpy as jnp
from jax import lax
import numpy as np

D_MODEL = 1024
BATCH = 1
SEQ = 2048
DEPTH = 1

CHUNK = 64
EPS = 1e-6

GDN_HEADS = 4
GDN_DK = 128
GDN_DV = 128
GDN_QK_W = GDN_HEADS * GDN_DK
GDN_V_W = GDN_HEADS * GDN_DV
CONV_WIDTH = 4
CONV_CH = 2 * GDN_QK_W + GDN_V_W

ATTN_Q_HEADS = 8
ATTN_KV_HEADS = 2
ATTN_GROUP = ATTN_Q_HEADS // ATTN_KV_HEADS
ATTN_HEAD_DIM = 64
ATTN_Q_W = ATTN_Q_HEADS * ATTN_HEAD_DIM
ATTN_KV_W = ATTN_KV_HEADS * ATTN_HEAD_DIM
WINDOW = 128
WINDOW_CHUNKS = WINDOW // CHUNK

MIX_W = GDN_V_W + ATTN_Q_W
D_FF = 4 * D_MODEL

IN_SIZES = [GDN_QK_W, GDN_QK_W, GDN_V_W, GDN_V_W, GDN_HEADS, GDN_HEADS, ATTN_Q_W, ATTN_KV_W, ATTN_KV_W]
IN_COLS = sum(IN_SIZES)
IN_SPLITS = [sum(IN_SIZES[:i + 1]) for i in range(len(IN_SIZES) - 1)]

kernel_name = 'hybrid_gdn_swa_streaming_block'

def _rmsnorm(x, w):
    xf = x.astype(jnp.float32)
    y = xf * lax.rsqrt(jnp.mean(xf * xf, axis=-1, keepdims=True) + EPS)
    return (y * w.astype(jnp.float32)).astype(x.dtype)

def _l2norm(x):
    return x * lax.rsqrt(jnp.sum(x * x, axis=-1, keepdims=True) + EPS)

def _causal_conv(x, w):
    return lax.conv_general_dilated(
        x, w[:, None, :].astype(x.dtype), window_strides=(1,),
        padding=[(CONV_WIDTH - 1, 0)], dimension_numbers=('NWC', 'WIO', 'NWC'),
        feature_group_count=x.shape[-1])

def _gated_delta_rule(q, k, v, g, beta):
    f32 = jnp.float32
    B, S, H, DK = q.shape
    DV = v.shape[-1]
    n = S // CHUNK
    q = _l2norm(q.astype(f32)) * (DK ** -0.5)
    k = _l2norm(k.astype(f32))
    v = v.astype(f32)

    def chunks(t):
        return t.reshape(B, n, CHUNK, H, -1).transpose(0, 3, 1, 2, 4)

    q, k, v = chunks(q), chunks(k), chunks(v)
    g = g.astype(f32).reshape(B, n, CHUNK, H).transpose(0, 3, 1, 2)
    beta = beta.astype(f32).reshape(B, n, CHUNK, H).transpose(0, 3, 1, 2)
    gc = jnp.cumsum(g, axis=-1)

    idx = jnp.arange(CHUNK)
    incl = idx[:, None] >= idx[None, :]
    strict = idx[:, None] > idx[None, :]
    decay = jnp.exp(jnp.where(incl, gc[..., :, None] - gc[..., None, :], -jnp.inf))

    kb = k * beta[..., None]
    a = jnp.where(strict, jnp.einsum('bhncd,bhnsd->bhncs', kb, k) * decay, 0.0)
    lower = a + jnp.eye(CHUNK, dtype=f32)
    u = lax.linalg.triangular_solve(lower, v * beta[..., None], left_side=True,
                                    lower=True, unit_diagonal=True)
    w = lax.linalg.triangular_solve(lower, kb * jnp.exp(gc)[..., None], left_side=True,
                                    lower=True, unit_diagonal=True)
    qk = jnp.einsum('bhncd,bhnsd->bhncs', q, k) * decay
    q_dec = q * jnp.exp(gc)[..., None]
    k_dec = k * jnp.exp(gc[..., -1:] - gc)[..., None]
    g_last = jnp.exp(gc[..., -1])

    xs = tuple(jnp.moveaxis(t, 2, 0) for t in (qk, q_dec, k_dec, u, w, g_last))

    def step(state, inp):
        qk_i, q_dec_i, k_dec_i, u_i, w_i, gl_i = inp
        v_new = u_i - jnp.einsum('bhcd,bhde->bhce', w_i, state)
        o = (jnp.einsum('bhcd,bhde->bhce', q_dec_i, state)
             + jnp.einsum('bhcs,bhse->bhce', qk_i, v_new))
        state = state * gl_i[..., None, None] + jnp.einsum('bhcd,bhce->bhde', k_dec_i, v_new)
        return state, o

    state0 = jnp.zeros((B, H, DK, DV), f32)
    _, o = lax.scan(step, state0, xs)
    return o.transpose(1, 0, 3, 2, 4).reshape(B, S, H, DV)

def _banded(t):
    P = WINDOW_CHUNKS - 1
    n = t.shape[1]
    tp = jnp.pad(t, [(0, 0), (P, 0)] + [(0, 0)] * (t.ndim - 2))
    return jnp.concatenate([tp[:, o:o + n] for o in range(WINDOW_CHUNKS)], axis=2)

def _sliding_window_attention(q, k, v, sinks, q_norm_w, k_norm_w):
    f32 = jnp.float32
    B, S, _, d = q.shape
    n = S // CHUNK
    P = WINDOW_CHUNKS - 1
    WC = WINDOW_CHUNKS * CHUNK
    q = _rmsnorm(q, q_norm_w)
    k = _rmsnorm(k, k_norm_w)
    qc = q.reshape(B, n, CHUNK, ATTN_KV_HEADS, ATTN_GROUP, d)
    kb = _banded(k.reshape(B, n, CHUNK, ATTN_KV_HEADS, d))
    vb = _banded(v.reshape(B, n, CHUNK, ATTN_KV_HEADS, d))

    s = jnp.einsum('bnqhgd,bnkhd->bnhgqk', qc, kb).astype(f32) * (d ** -0.5)

    qi = jnp.arange(CHUNK)[:, None]
    kj = jnp.arange(WC)[None, :]
    dist = jnp.abs(qi + P * CHUNK - kj).astype(f32)
    slopes = jnp.exp2(-8.0 * jnp.arange(1, ATTN_Q_HEADS + 1, dtype=f32) / ATTN_Q_HEADS)
    slopes = slopes.reshape(ATTN_KV_HEADS, ATTN_GROUP)
    s = s - slopes[:, :, None, None] * dist

    chunk_idx = jnp.arange(n)[:, None]
    valid = (chunk_idx - P + kj // CHUNK) >= 0
    s = jnp.where(valid[None, :, None, None, None, :], s, -jnp.inf)

    sink = sinks.astype(f32).reshape(ATTN_KV_HEADS, ATTN_GROUP)[None, None, :, :, None, None]
    m = jnp.maximum(jnp.max(s, axis=-1, keepdims=True), sink)
    p = jnp.exp(s - m)
    p = p / (jnp.sum(p, axis=-1, keepdims=True) + jnp.exp(sink - m))
    o = jnp.einsum('bnhgqk,bnkhd->bnqhgd', p.astype(v.dtype), vb)
    return o.reshape(B, S, ATTN_Q_W)

def setup_inputs(seed: int = 0) -> dict:
    key = jax.random.key(seed)
    ks = jax.random.split(key, 16)
    f32 = jnp.float32
    x = jax.random.normal(ks[0], (BATCH, SEQ, D_MODEL), f32)
    norm1_w = 1.0 + 0.02 * jax.random.normal(ks[1], (DEPTH, D_MODEL), f32)
    w_in = jax.random.normal(ks[2], (DEPTH, D_MODEL, IN_COLS), f32) * D_MODEL ** -0.5
    conv_w = jax.random.normal(ks[3], (DEPTH, CONV_WIDTH, CONV_CH), f32) * CONV_WIDTH ** -0.5
    a_log = jnp.log(jax.random.uniform(ks[4], (DEPTH, GDN_HEADS), f32, minval=1.0, maxval=16.0))
    dt = jnp.exp(jax.random.uniform(ks[5], (DEPTH, GDN_HEADS), f32,
                                    minval=float(np.log(1e-3)), maxval=float(np.log(1e-1))))
    dt_bias = dt + jnp.log(-jnp.expm1(-dt))
    gdn_norm_w = 1.0 + 0.02 * jax.random.normal(ks[6], (DEPTH, GDN_DV), f32)
    q_norm_w = 1.0 + 0.02 * jax.random.normal(ks[7], (DEPTH, ATTN_HEAD_DIM), f32)
    k_norm_w = 1.0 + 0.02 * jax.random.normal(ks[8], (DEPTH, ATTN_HEAD_DIM), f32)
    sinks = 0.5 * jax.random.normal(ks[9], (DEPTH, ATTN_Q_HEADS), f32)
    w_out = jax.random.normal(ks[10], (DEPTH, MIX_W, D_MODEL), f32) * MIX_W ** -0.5
    norm2_w = 1.0 + 0.02 * jax.random.normal(ks[11], (DEPTH, D_MODEL), f32)
    w1 = jax.random.normal(ks[12], (DEPTH, D_MODEL, D_FF), f32) * D_MODEL ** -0.5
    w2 = jax.random.normal(ks[13], (DEPTH, D_FF, D_MODEL), f32) * D_FF ** -0.5
    return {'x': x, 'norm1_w': norm1_w, 'w_in': w_in, 'conv_w': conv_w, 'a_log': a_log,
            'dt_bias': dt_bias, 'gdn_norm_w': gdn_norm_w, 'q_norm_w': q_norm_w,
            'k_norm_w': k_norm_w, 'sinks': sinks, 'w_out': w_out, 'norm2_w': norm2_w,
            'w1': w1, 'w2': w2}

def reference(x, norm1_w, w_in, conv_w, a_log, dt_bias, gdn_norm_w, q_norm_w, k_norm_w,
              sinks, w_out, norm2_w, w1, w2):
    f32 = jnp.float32
    B, S, _ = x.shape
    for l in range(DEPTH):
        h = _rmsnorm(x, norm1_w[l])
        proj = h @ w_in[l]
        gq, gk, gv, gz, gb, ga, aq, ak, av = jnp.split(proj, IN_SPLITS, axis=-1)

        qkv = jax.nn.silu(_causal_conv(jnp.concatenate([gq, gk, gv], axis=-1), conv_w[l]))
        cq, ck, cv = jnp.split(qkv, [GDN_QK_W, 2 * GDN_QK_W], axis=-1)
        beta = jax.nn.sigmoid(gb.astype(f32))
        g = -jnp.exp(a_log[l].astype(f32)) * jax.nn.softplus(ga.astype(f32) + dt_bias[l].astype(f32))
        o_gdn = _gated_delta_rule(cq.reshape(B, S, GDN_HEADS, GDN_DK),
                                  ck.reshape(B, S, GDN_HEADS, GDN_DK),
                                  cv.reshape(B, S, GDN_HEADS, GDN_DV), g, beta)
        z = gz.astype(f32).reshape(B, S, GDN_HEADS, GDN_DV)
        o_gdn = (o_gdn * lax.rsqrt(jnp.mean(o_gdn * o_gdn, axis=-1, keepdims=True) + EPS)
                 * gdn_norm_w[l].astype(f32) * jax.nn.silu(z))
        o_gdn = o_gdn.astype(x.dtype).reshape(B, S, GDN_V_W)

        o_attn = _sliding_window_attention(
            aq.reshape(B, S, ATTN_Q_HEADS, ATTN_HEAD_DIM),
            ak.reshape(B, S, ATTN_KV_HEADS, ATTN_HEAD_DIM),
            av.reshape(B, S, ATTN_KV_HEADS, ATTN_HEAD_DIM),
            sinks[l], q_norm_w[l], k_norm_w[l])

        mix = jnp.concatenate([o_gdn, o_attn.astype(x.dtype)], axis=-1)
        x = x + mix @ w_out[l]

        h2 = _rmsnorm(x, norm2_w[l])
        x = x + jnp.square(jax.nn.relu(h2 @ w1[l])) @ w2[l]
    return x


_drawn_inputs = setup_inputs


def setup_inputs(seed=0):
    import zlib

    import numpy as np

    out = dict(_drawn_inputs(seed))
    spreads = {}
    factors = {'norm1_w': 3.592,
     'gdn_norm_w': 6.614,
     'q_norm_w': 8.0,
     'k_norm_w': 8.0,
     'sinks': 6.464,
     'norm2_w': 10.592}
    for name, (base, spread) in spreads.items():
        noise = np.random.default_rng([zlib.crc32(name.encode()), seed]).standard_normal(out[name].shape)
        drawn = base * np.exp(spread * noise) if base else spread * noise
        out[name] = __import__('jax').numpy.asarray(drawn.astype(out[name].dtype))
    for name, factor in factors.items():
        out[name] = (out[name] * factor).astype(out[name].dtype)
    return out
```

```python
import math

from contextlib import ExitStack

import numpy as np

import concourse.bass as bass
from concourse import mybir

F32 = mybir.dt.float32
F32R = mybir.dt.float32r
ALU = mybir.AluOpType
ACT = mybir.ActivationFunctionType
AX = mybir.AxisListType

P = 128
D = 1024
SEQ = 2048
TOK = 512
GROUPS = SEQ // TOK
TILES = TOK // P
KT = D // P
HEADS = 4
PAIRS = 4
HD = 64
KEYS = 192
LEVELS = 6
EPS = 1e-6
NEG = -1e30

CONV, GATE = 12, 4
U_BA, U_AV, U_AK, U_AQ = 16, 17, 18, 19
U_PAD, U_OUT, U_MLP = 23, 24, 32
UNITS = 96
NORMS = 13
SLOTS = 4

C_N1, C_N2, C_CONV, C_GN, C_QN, C_KN, C_ALOG, C_DT, C_SINK = 0, 8, 16, 64, 65, 66, 67, 68, 69
N_PAR = C_SINK + 2 * PAIRS
K_ID, K_ONE, K_MEAN, K_MEANX, K_HALF, K_CAUS, K_M0, K_LEV, K_SEL = 0, 1, 2, 3, 4, 5, 6, 7, 13
N_CONST = K_SEL + 2 * HEADS


class Signal:

    def __init__(self, sem, per_group, credit=0, step=1):
        self.sem, self.per_group, self.credit, self.step = sem, per_group, credit, step

    def after(self, g, n):
        return g * (self.per_group * self.step) + n * self.step + self.credit


def build(nc, x, w, par, con, bias, out):
    with ExitStack() as ctx:
        def sb(name, shape, dt=F32, scope=ctx):
            return scope.enter_context(nc.sbuf_tensor(name, shape, dt))

        def signal(name, per_group, credit=0, step=1):
            return Signal(ctx.enter_context(nc.semaphore(name)), per_group, credit, step)

        stage = sb("stage", [P, SLOTS, KT, P])
        w_h = sb("w_h", [P, 2, KT, P], F32R)
        w_l = sb("w_l", [P, 2, KT, P], F32R)
        xs = sb("xs", [P, KT, TOK])
        h_h = sb("h_h", [P, KT, TOK], F32R)
        h_l = sb("h_l", [P, KT, TOK], F32R)
        aq = sb("aq", [P, PAIRS, TOK])
        kn = sb("kn", [P, HD + TOK])
        vt = sb("vt", [P, 1 + TILES, P])
        state = sb("state", [P, HEADS, P])
        tail = sb("tail", [P, CONV, 3])
        row = sb("row", [64, TOK])
        cst = sb("cst", [P, N_CONST, P])
        bia = sb("bia", [P, 2, PAIRS, 2, KEYS])
        prm = sb("prm", [P, N_PAR])
        nalog = sb("nalog", [P, 1])
        nsink = sb("nsink", [P, 2 * PAIRS])
        eps = sb("eps", [P, 1])
        small = sb("small", [P, 64])
        with ExitStack() as s:
            ff_h = sb("ff_h", [P, 16, TOK], F32R, s)
            ff_l = sb("ff_l", [P, 16, TOK], F32R, s)
        qkvz = sb("qkvz", [P, 16, TOK])
        with ExitStack() as s:
            raw = sb("raw", [P, 2, 3 + TOK], F32, s)
            cy = sb("cy", [P, 2, TOK], F32, s)
            nq = sb("nq", [P, 2, TOK], F32, s)
            rr = sb("rr", [P, 2, TOK], F32, s)
            akr = sb("akr", [P, TOK], F32, s)
            avr = sb("avr", [P, TOK], F32, s)
            rw = sb("rw", [P, 4, TOK], F32, s)
        eg, dta, dt_, db, at_, xi, ti, yi, kb, kd, vb, qk, qd, wt, vn = (
            sb(n, [P, HEADS, P]) for n in "eg dta dt db at xi ti yi kb kd vb qk qd wt vn".split())
        sb("rest_of_hidden", [P, TOK])
        with ExitStack() as s:
            sq = sb("sq", [P, 2, TOK], F32, s)
            acc = sb("acc", [P, TOK], F32, s)
            rt = sb("rt", [P, TOK], F32, s)
            ht = sb("ht", [P, 2, TOK], F32, s)
            fb = sb("fb", [P, 2, TOK], F32, s)
            ff = sb("ff", [P, 2, TOK], F32, s)
        ss = sb("ss", [P, 2, 2, KEYS])
        pp = sb("pp", [P, 2, 2, 256])
        pts = sb("pts", [P, 2, 2, 2, P])
        osq = sb("osq", [P, HEADS, P])
        ro = sb("ro", [P, HEADS, P])
        mx_ = sb("mx", [P, HEADS, P])

        ps = ctx.enter_context(nc.psum_tensor("ps", [P, 8, 512], F32))
        SC0, PT0, OV, R5, R6, R7 = 0, 2, 4, 5, 6, 7

        def heads(b):
            return ps[:, b, :].rearrange("p (h c) -> p h c", h=HEADS)

        I = cst[:, K_ID, :]

        def wide(v):
            return v.unsqueeze(2).to_broadcast([P, HEADS, P])

        def per_head(m):
            return m.unsqueeze(1).to_broadcast([P, HEADS, P])

        const_loaded = ctx.enter_context(nc.semaphore("const_loaded"))
        init_done = ctx.enter_context(nc.semaphore("init_done"))
        init_act = ctx.enter_context(nc.semaphore("init_act"))
        w_loaded = [signal(f"w_loaded{i}", UNITS // SLOTS, step=16) for i in range(SLOTS)]
        w_hi = signal("w_hi", UNITS)
        w_lo = signal("w_lo", UNITS, credit=SLOTS)
        unit_done = signal("unit_done", UNITS, credit=2)
        x_loaded = signal("x_loaded", 1, step=16)
        y_stored = signal("y_stored", KT, step=16)
        sq_ready = signal("sq_ready", 16)
        acc_ready = signal("acc_ready", 16)
        ns_sum = signal("ns_sum", 2)
        rt_ln = signal("rt_ln", 2)
        rt_ready = signal("rt_ready", 2)
        ht_ready = signal("ht_ready", 16)
        hh_ready = signal("hh_ready", 16)
        h_ready = signal("h_ready", 16)
        raw_ready = signal("raw_ready", 3 * CONV, credit=6)
        tap_done = signal("tap_done", 4 * CONV)
        silu_done = signal("silu_done", CONV, credit=2)
        z_ready = signal("z_ready", GATE)
        copied = signal("copied", 6)
        nsq_ready = signal("nsq_ready", NORMS)
        nsum_done = signal("nsum_done", NORMS)
        nln_done = signal("nln_done", NORMS)
        nrr_ready = signal("nrr_ready", NORMS)
        normed = signal("normed", NORMS + 1)
        row_act = signal("row_act", 4)
        row_dve = signal("row_dve", 15)
        vt_sum = signal("vt_sum", 1)
        vt_ready = signal("vt_ready", 2)
        B = {n: signal(n, TILES) for n in
             ("p_rowt p_gr p_br p_gg p_kt p_vt p_kq p_wt p_vv p_oo p_su p_on "
              "tok ng dta_r d2 c1 db_r at_r x0a qk_r vb_r kb_r kd_r o1 o2 mlo "
              "egt eg_r dt_r c2 wtc vnc osq_r oln orr mhi qd_r").split()}
        p_y = signal("p_y", TILES * LEVELS)
        p_z = signal("p_z", TILES * LEVELS)
        p_t = signal("p_t", TILES * LEVELS)
        y_ready = signal("y_ready", TILES * LEVELS)
        x_ready = signal("x_ready", TILES * (LEVELS + 1))
        t_ready = signal("t_ready", TILES * LEVELS)
        s_ready = signal("s_ready", TILES * HEADS)
        A = {n: signal(n, TILES * PAIRS) for n in
             "p_sc p_pt ss_r amax nmax sdiff den_r rden p_ready es_r ptc".split()}
        p_ov = signal("p_ov", TILES)
        ahi = signal("ahi", TILES)
        alo = signal("alo", TILES)
        pads = signal("pads", 1)
        res = signal("res", KT + 2 * KT, credit=1)
        fb_ready = signal("fb_ready", 32)
        fh_ready = signal("fh_ready", 32)
        fp_ready = signal("fp_ready", 32, credit=2)
        ff_ready = signal("ff_ready", 32, credit=2)

        block = ctx.enter_context(nc.Block())

        @block.sync
        def _(sp):
            def load(u, s, dst_wait=None):
                sp.dma_start(stage[:, s], w[u].rearrange("p (k m) -> p k m", k=KT)).then_inc(w_loaded[s].sem, 16)

            sp.dma_start(cst[:], con).then_inc(const_loaded, 16)
            sp.dma_start(prm[:], par).then_inc(const_loaded, 16)
            sp.dma_start(bia[:], bias.rearrange("p (v j e k) -> p v j e k", v=2, j=PAIRS, e=2)).then_inc(const_loaded, 16)
            with sp.Fori(0, GROUPS) as g:
                with sp.Fori(0, UNITS // SLOTS) as i:
                    for s in range(SLOTS):
                        sp.wait_ge(w_lo.sem, w_lo.after(g, i * SLOTS + (s + 1 - SLOTS)))
                        load(i * SLOTS + s, s)
            sp.wait_ge(w_lo.sem, w_lo.after(GROUPS, 1 - SLOTS))
            load(0, 0)

        @block.gpsimd
        def _(pool):
            pool.dma_start(xs[:], x[0]).then_inc(x_loaded.sem, 16)
            with pool.Fori(0, GROUPS) as g:
                for t in range(TILES):
                    tile = slice(t * P, t * P + P)
                    pool.wait_ge(B["eg_r"].sem, B["eg_r"].after(g, t + 1))
                    if t == 0:
                        pool.wait_ge(normed.sem, normed.after(g, NORMS + 1))
                    nc.gpsimd.tensor_tensor(qd[:], qkvz[:, 0:4, tile], eg[:], ALU.mult).then_inc(B["qd_r"].sem, 1)
                for m in range(KT):
                    pool.wait_ge(res.sem, res.after(g, 2 * KT + m + 1))
                    pool.nop(nofuse=True)
                    pool.dma_start(out[g, :, m], xs[:, m]).then_inc(y_stored.sem, 16)
                pool.wait_ge(y_stored.sem, y_stored.after(g, KT))
                pool.nop(nofuse=True)
                pool.dma_start(xs[:], x[(g + 1) % GROUPS]).then_inc(x_loaded.sem, 16)
            pool.wait_ge(x_loaded.sem, x_loaded.after(GROUPS, 1))

        @block.scalar
        def _(act):
            def split_hi(g, u, n=0):
                s, b = n % SLOTS, n % 2
                act.wait_ge(w_loaded[s].sem, w_loaded[s].after(g, u_div(u, n) + 1))
                act.wait_ge(unit_done.sem, unit_done.after(g, u + (n - 1)))
                act.copy(w_h[:, b], stage[:, s]).then_inc(w_hi.sem, 1)

            def rms_square(g, which, k):
                if which == 1:
                    act.wait_ge(res.sem, res.after(g, k + 1))
                elif k == 0:
                    act.wait_ge(x_loaded.sem, x_loaded.after(g, 1))
                if k >= 2:
                    act.wait_ge(acc_ready.sem, acc_ready.after(g, 8 * which + k - 1))
                act.activation(sq[:, k % 2], xs[:, k], ACT.Square).then_inc(sq_ready.sem, 1)

            def rms_root(g, which):
                act.wait_ge(ns_sum.sem, ns_sum.after(g, which + 1))
                act.activation(rt[:], ps[:, OV, :], ACT.Ln, bias=eps[:, 0:1]).then_inc(rt_ln.sem, 1)
                act.wait_ge(rt_ln.sem, rt_ln.after(g, which + 1))
                act.activation(rt[:], rt[:], ACT.Exp, scale=-0.5).then_inc(rt_ready.sem, 1)
                for k in range(KT):
                    act.wait_ge(ht_ready.sem, ht_ready.after(g, 8 * which + k + 1))
                    act.copy(h_h[:, k], ht[:, k % 2]).then_inc(hh_ready.sem, 1)

            act.wait_ge(const_loaded, 48)
            act.wait_ge(init_done, 1)
            act.preload_act_table_set("natural_log_exp_and_others")
            act.activation(nalog[32:36], prm[32:36, C_ALOG:C_ALOG + 1], ACT.Exp).then_inc(init_act, 1)
            act.sem_inc(raw_ready.sem, 6)
            act.sem_inc(silu_done.sem, 2)
            split_hi(0, 0)

            with act.Fori(0, GROUPS) as g:
                for k in range(KT):
                    rms_square(g, 0, k)
                rms_root(g, 0)
                act.preload_act_table_set("silu_and_others")

                def silu(i, s):
                    m = i * 4 + s
                    act.wait_ge(tap_done.sem, tap_done.after(g, m * 4 + 4))
                    act.activation(qkvz[:, m, :], cy[:, s % 2], ACT.Silu).then_inc(silu_done.sem, 1)

                with act.Fori(0, CONV // 4) as i:
                    for s in range(4):
                        split_hi(g, i * 4, s + 1)
                        act.wait_ge(unit_done.sem, unit_done.after(g, i * 4 + s + 1))
                        act.copy(raw[:, s % 2, 3:], ps[:, s % 2, :]).then_inc(raw_ready.sem, 1)
                        act.copy(raw[:, s % 2, 0:3], tail[:, i * 4 + s, :]).then_inc(raw_ready.sem, 1)
                        act.wait_ge(raw_ready.sem, raw_ready.after(g, (i * 4 + s) * 3 + 2))
                        act.nop(nofuse=True)
                        act.copy(tail[:, i * 4 + s, :], ps[:, s % 2, TOK - 3:]).then_inc(raw_ready.sem, 1)
                        if s:
                            silu(i, s - 1)
                    silu(i, 3)
                for m in range(GATE):
                    split_hi(g, CONV, m + 1)
                    act.wait_ge(unit_done.sem, unit_done.after(g, CONV + m + 1))
                    act.activation(qkvz[:, 12 + m, :], ps[:, m % 2, :], ACT.Silu).then_inc(z_ready.sem, 1)

                act.preload_act_table_set("natural_log_exp_and_others")

                def norm_root(n):
                    act.wait_ge(nsum_done.sem, nsum_done.after(g, n + 1))
                    act.activation(rr[:, n % 2], ps[:, R5 + n % 2, :], ACT.Ln, bias=eps[:, 0:1]).then_inc(nln_done.sem, 1)
                    act.wait_ge(nln_done.sem, nln_done.after(g, n + 1))
                    act.activation(rr[:, n % 2], rr[:, n % 2], ACT.Exp, scale=-0.5).then_inc(nrr_ready.sem, 1)

                split_hi(g, U_BA, 1)
                act.wait_ge(unit_done.sem, unit_done.after(g, U_BA + 1))
                act.activation(row[0:4], ps[0:4, 0, :], ACT.Exp, scale=-1.0).then_inc(row_act.sem, 1)
                act.activation(rw[32:36, 0], ps[32:36, 0, :], ACT.Identity, bias=prm[32:36, C_DT:C_DT + 1]).then_inc(row_act.sem, 1)
                norm_root(0)
                split_hi(g, U_BA, 2)
                act.wait_ge(unit_done.sem, unit_done.after(g, U_AV + 1))
                act.copy(avr[:], ps[:, 1, :]).then_inc(copied.sem, 1)
                act.wait_ge(row_dve.sem, row_dve.after(g, 3))
                act.activation(rw[32:36, 1], rw[32:36, 1], ACT.Exp, scale=-1.0).then_inc(row_act.sem, 1)
                norm_root(1)
                norm_root(2)
                split_hi(g, U_BA, 3)
                act.wait_ge(unit_done.sem, unit_done.after(g, U_AK + 1))
                act.copy(akr[:], ps[:, 0, :]).then_inc(copied.sem, 1)
                act.wait_ge(row_dve.sem, row_dve.after(g, 4))
                act.activation(rw[32:36, 3], rw[32:36, 2], ACT.Ln).then_inc(row_act.sem, 1)
                norm_root(3)
                norm_root(4)
                act.copy(vt[:, 0], vt[:, TILES]).then_inc(vt_ready.sem, 1)
                act.wait_ge(vt_ready.sem, vt_ready.after(g, 1))
                act.wait_ge(vt_sum.sem, vt_sum.after(g, 1))
                act.copy(vt[:, 1:], heads(OV)).then_inc(vt_ready.sem, 1)
                for j in range(PAIRS):
                    split_hi(g, U_BA, 4 + j)
                    act.wait_ge(unit_done.sem, unit_done.after(g, U_AQ + j + 1))
                    act.copy(aq[:, j], ps[:, (U_AQ + j) % 2, :]).then_inc(copied.sem, 1)
                    norm_root(5 + 2 * j)
                    norm_root(6 + 2 * j)
                split_hi(g, U_BA, 8)

                def exps(t, j):
                    n = t * PAIRS + j
                    b = j % 2
                    o = 32 * b
                    act.wait_ge(A["nmax"].sem, A["nmax"].after(g, n + 1))
                    if n == 0:
                        act.wait_ge(pads.sem, pads.after(g, 1))
                    for e in range(2):
                        act.activation(pp[:, b, e, HD:], ss[:, b, e], ACT.Exp, bias=small[:, o + 2 + e:o + 3 + e],
                                       accum_out=small[:, o + 4 + e:o + 5 + e])
                    act.wait_ge(A["sdiff"].sem, A["sdiff"].after(g, n + 1))
                    act.activation(small[:, o + 8:o + 10], small[:, o + 6:o + 8], ACT.Exp).then_inc(A["es_r"].sem, 1)

                def pt_copy(t, j):
                    n = t * PAIRS + j
                    act.wait_ge(A["p_pt"].sem, A["p_pt"].after(g, n + 1))
                    act.copy(pts[:, j % 2], ps[:, PT0 + j % 2, :].rearrange("p (e c k) -> p e c k", e=2, c=2)).then_inc(A["ptc"].sem, 1)

                def t_copy(t, l):
                    n = t * LEVELS + l
                    act.wait_ge(p_t.sem, p_t.after(g, n + 1))
                    act.copy(ti[:], heads(R6)).then_inc(t_ready.sem, 1)

                for t in range(TILES):
                    tile = slice(t * P, t * P + P)

                    def w(s, n=t + 1):
                        act.wait_ge(s.sem, s.after(g, n))

                    exps(t, 0)
                    w(B["tok"])
                    act.activation(small[:, 28:32], small_tok(small)[:, 4:8], ACT.Exp).then_inc(B["egt"].sem, 1)
                    w(B["d2"])
                    act.activation(eg[:], heads(R6), ACT.Exp).then_inc(B["eg_r"].sem, 1)
                    for h in range(HEADS):
                        a = act.activation(dt_[:, h], dta[:, h], ACT.Exp, bias=small[:, 12 + h:13 + h])
                    a.then_inc(B["dt_r"].sem, 1)
                    act.activation(small[:, 20:24], small[:, 24:28], ACT.Exp).then_inc(B["c2"].sem, 1)
                    t_copy(t, 0)
                    t_copy(t, 1)
                    exps(t, 1)
                    pt_copy(t, 0)
                    t_copy(t, 2)
                    exps(t, 2)
                    pt_copy(t, 1)
                    t_copy(t, 3)
                    exps(t, 3)
                    pt_copy(t, 2)
                    t_copy(t, 4)
                    pt_copy(t, 3)
                    t_copy(t, 5)
                    w(p_ov)
                    act.copy(h_h[:, 4:8, tile], heads(OV)).then_inc(ahi.sem, 1)
                    w(B["p_wt"])
                    act.copy(wt[:], heads(R6)).then_inc(B["wtc"].sem, 1)
                    w(B["p_vv"])
                    act.copy(vn[:], heads(R7)).then_inc(B["vnc"].sem, 1)
                    w(B["p_oo"])
                    act.activation(osq[:], heads(R5), ACT.Square).then_inc(B["osq_r"].sem, 1)
                    w(B["p_on"])
                    act.activation(ro[:], heads(R7), ACT.Ln, bias=eps[:, 0:1]).then_inc(B["oln"].sem, 1)
                    w(B["oln"])
                    act.activation(ro[:], ro[:], ACT.Exp, scale=-0.5).then_inc(B["orr"].sem, 1)
                    w(B["o2"])
                    act.copy(h_h[:, 0:4, tile], mx_[:]).then_inc(B["mhi"].sem, 1)

                for m in range(KT):
                    split_hi(g, U_OUT, m + 1)
                    if m:
                        rms_square(g, 1, m - 1)
                rms_square(g, 1, KT - 1)
                rms_root(g, 1)
                for half in range(2):
                    with act.Fori(0, 4) as i:
                        for s in range(4):
                            u = U_MLP + 32 * half
                            n = half * 16 + s
                            split_hi(g, i * 4 + u, s + 1)
                            act.wait_ge(unit_done.sem, unit_done.after(g, i * 4 + u + s + 1))
                            act.wait_ge(ff_ready.sem, ff_ready.after(g, i * 4 + n - 1))
                            act.activation(fb[:, s % 2], ps[:, s % 2, :], ACT.Relu).then_inc(fb_ready.sem, 1)
                            act.wait_ge(fb_ready.sem, fb_ready.after(g, i * 4 + n + 1))
                            act.activation(ff_h[:, i * 4 + s, :], fb[:, s % 2], ACT.Square).then_inc(fh_ready.sem, 1)
                    with act.Fori(0, 4) as i:
                        for s in range(4):
                            split_hi(g, i * 4 + (U_MLP + 16 + 32 * half), s + 1)

        @block.vector
        def _(dve):
            def own(sig, g, n):
                dve.wait_ge(sig.sem, sig.after(g, n))

            def split_lo(g, u, n=0):
                s, b = n % SLOTS, n % 2
                dve.wait_ge(w_hi.sem, w_hi.after(g, u + (n + 1)))
                dve.tensor_tensor(w_l[:, b], stage[:, s], w_h[:, b].bitcast(F32), ALU.subtract).then_inc(w_lo.sem, 1)

            def acc_add(g, which, k):
                n = 8 * which + k
                dve.wait_ge(sq_ready.sem, sq_ready.after(g, n + 1))
                if k == 0:
                    dve.tensor_copy(acc[:], sq[:, 0]).then_inc(acc_ready.sem, 1)
                else:
                    own(acc_ready, g, n)
                    dve.tensor_tensor(acc[:], acc[:], sq[:, k % 2], ALU.add).then_inc(acc_ready.sem, 1)

            def rms_apply(g, which):
                col = C_N2 if which else C_N1
                dve.wait_ge(rt_ready.sem, rt_ready.after(g, which + 1))
                for k in range(KT + 1):
                    n = 8 * which + k
                    if 2 <= k < KT:
                        own(h_ready, g, n - 1)
                    if k < KT:
                        dve.scalar_tensor_tensor(out=ht[:, k % 2], in0=xs[:, k], scalar=prm[:, col + k:col + k + 1],
                                                 in1=rt[:], op0=ALU.mult, op1=ALU.mult).then_inc(ht_ready.sem, 1)
                    if k:
                        dve.wait_ge(hh_ready.sem, hh_ready.after(g, n))
                        dve.tensor_tensor(h_l[:, k - 1], ht[:, (k - 1) % 2], h_h[:, k - 1].bitcast(F32),
                                          ALU.subtract).then_inc(h_ready.sem, 1)

            dve.memset(eps[:], EPS).then_inc(init_done, 1)
            dve.memset(state[:], 0.0)
            dve.memset(tail[:], 0.0)
            dve.memset(row[:], 0.0)
            dve.memset(kn[:], 0.0)
            dve.memset(vt[:], 0.0)
            dve.wait_ge(const_loaded, 48)
            dve.tensor_scalar(nsink[:], prm[:, C_SINK:C_SINK + 8], -1.0, None, ALU.mult)
            dve.wait_ge(init_act, 1)
            dve.tensor_scalar(nalog[32:36], nalog[32:36], -1.0, None, ALU.mult).then_inc(init_done, 1)
            dve.wait_ge(init_done, 2)
            dve.sem_inc(w_lo.sem, SLOTS)
            dve.sem_inc(res.sem, 1)
            dve.sem_inc(fp_ready.sem, 2)
            dve.sem_inc(ff_ready.sem, 2)
            split_lo(0, 0)

            with dve.Fori(0, GROUPS) as g:
                for k in range(KT):
                    acc_add(g, 0, k)
                rms_apply(g, 0)
                with dve.Fori(0, CONV // 4) as i:
                    for s in range(4):
                        m = i * 4 + s
                        split_lo(g, i * 4, s + 1)
                        dve.wait_ge(raw_ready.sem, raw_ready.after(g, m * 3 + 3))
                        dve.wait_ge(silu_done.sem, silu_done.after(g, m - 1))
                        dve.tensor_scalar(cy[:, s % 2], raw[:, s % 2, 0:TOK], convw(prm, m, 0), None,
                                          ALU.mult).then_inc(tap_done.sem, 1)
                        for j in range(1, 4):
                            own(tap_done, g, m * 4 + j)
                            dve.scalar_tensor_tensor(out=cy[:, s % 2], in0=raw[:, s % 2, j:j + TOK],
                                                     scalar=convw(prm, m, j), in1=cy[:, s % 2],
                                                     op0=ALU.mult, op1=ALU.add).then_inc(tap_done.sem, 1)
                for m in range(GATE):
                    split_lo(g, CONV, m + 1)

                def src(n):
                    return qkvz[:, n, :] if n < 8 else akr[:] if n == 8 else aq[:, n - 9]

                def norm_square(n):
                    if n == 0:
                        dve.wait_ge(silu_done.sem, silu_done.after(g, 8))
                    if n >= 8:
                        dve.wait_ge(copied.sem, copied.after(g, n - 6))
                    dve.tensor_tensor(nq[:, n % 2], src(n), src(n), ALU.mult).then_inc(nsq_ready.sem, 1)

                def norm_apply(n):
                    dve.wait_ge(nrr_ready.sem, nrr_ready.after(g, n + 1))
                    dst = kn[:, HD:] if n == 8 else src(n)
                    scale = (float(P) ** -0.5 if n < 4 else 1.0 if n < 8 else
                             prm[:, C_KN:C_KN + 1] if n == 8 else prm[:, C_QN:C_QN + 1])
                    if n == 8:
                        dve.tensor_copy(kn[:, 0:HD], kn[:, TOK:]).then_inc(normed.sem, 1)
                        own(normed, g, 9)
                    dve.scalar_tensor_tensor(out=dst, in0=src(n), scalar=scale, in1=rr[:, n % 2],
                                             op0=ALU.mult, op1=ALU.mult).then_inc(normed.sem, 1)

                rd = [0]

                def row_step(ins):
                    ins.then_inc(row_dve.sem, 1)
                    rd[0] += 1
                    own(row_dve, g, rd[0])

                A4 = slice(32, 36)
                X, E, U, L = (rw[A4, i] for i in range(4))
                split_lo(g, U_BA, 1)
                norm_square(0)
                norm_square(1)
                dve.wait_ge(row_act.sem, row_act.after(g, 2))
                row_step(dve.tensor_scalar(row[0:4], row[0:4], 1.0, None, ALU.add))
                row_step(dve.reciprocal(row[0:4], row[0:4]))
                row_step(dve.scalar_tensor_tensor(out=E, in0=X, scalar=-1.0, in1=X, op0=ALU.mult, op1=ALU.max))
                norm_apply(0)
                norm_square(2)
                split_lo(g, U_BA, 2)
                norm_apply(1)
                norm_square(3)
                dve.wait_ge(row_act.sem, row_act.after(g, 3))
                row_step(dve.tensor_scalar(U, E, 1.0, None, ALU.add))
                norm_apply(2)
                norm_square(4)
                split_lo(g, U_BA, 3)
                norm_apply(3)
                norm_square(5)
                dve.wait_ge(row_act.sem, row_act.after(g, 4))
                row_step(dve.scalar_tensor_tensor(out=E, in0=U, scalar=-1.0, in1=E, op0=ALU.add, op1=ALU.subtract))
                row_step(dve.reciprocal(U, U))
                row_step(dve.tensor_tensor(E, E, U, ALU.mult))
                row_step(dve.tensor_tensor(L, L, E, ALU.subtract))
                row_step(dve.scalar_tensor_tensor(out=L, in0=X, scalar=0.0, in1=L, op0=ALU.max, op1=ALU.add))
                row_step(dve.tensor_scalar(L, L, nalog[A4], None, ALU.mult))
                row_step(dve.memset(E, 1.0))
                for t in range(TILES):
                    tile = slice(t * P, t * P + P)
                    row_step(dve.tensor_tensor_scan(row[A4, tile], rw[A4, 1, tile], rw[A4, 3, tile], 0.0,
                                                    ALU.mult, ALU.add))
                assert rd[0] == row_dve.per_group
                norm_apply(4)
                norm_square(6)
                for j in range(PAIRS):
                    split_lo(g, U_BA, 4 + j)
                    norm_apply(5 + 2 * j)
                    norm_square(7 + 2 * j) if 7 + 2 * j < NORMS else None
                    norm_apply(6 + 2 * j) if j < 3 else None
                    norm_square(8 + 2 * j) if 8 + 2 * j < NORMS else None
                norm_apply(12)
                dve.memset(pp[:, :, :, 0:HD], 0.0).then_inc(pads.sem, 1)
                split_lo(g, U_BA, 8)

                def scores(t, j):
                    n = t * PAIRS + j
                    b = j % 2
                    o = 32 * b
                    dve.wait_ge(A["p_sc"].sem, A["p_sc"].after(g, n + 1))
                    var = (g + 3) // 4 if t == 0 else 1
                    dve.scalar_tensor_tensor(out=ss[:, b], in0=ps[:, SC0:SC0 + 2, 0:KEYS], scalar=HD ** -0.5,
                                             in1=bia[:, var, j], op0=ALU.mult, op1=ALU.add).then_inc(A["ss_r"].sem, 1)
                    own(A["ss_r"], g, n + 1)
                    dve.tensor_reduce(small[:, o:o + 2], ss[:, b], AX.X, ALU.max).then_inc(A["amax"].sem, 1)
                    own(A["amax"], g, n + 1)
                    dve.scalar_tensor_tensor(out=small[:, o + 2:o + 4], in0=small[:, o:o + 2], scalar=-1.0,
                                             in1=nsink[:, 2 * j:2 * j + 2], op0=ALU.mult,
                                             op1=ALU.min).then_inc(A["nmax"].sem, 1)
                    own(A["nmax"], g, n + 1)
                    dve.tensor_tensor(small[:, o + 6:o + 8], small[:, o + 2:o + 4],
                                      nsink[:, 2 * j:2 * j + 2], ALU.subtract).then_inc(A["sdiff"].sem, 1)

                def softmax(t, j):
                    n = t * PAIRS + j
                    b = j % 2
                    o = 32 * b
                    dve.wait_ge(A["es_r"].sem, A["es_r"].after(g, n + 1))
                    dve.tensor_tensor(small[:, o + 10:o + 12], small[:, o + 4:o + 6], small[:, o + 8:o + 10],
                                      ALU.add).then_inc(A["den_r"].sem, 1)
                    own(A["den_r"], g, n + 1)
                    dve.reciprocal(small[:, o + 10:o + 12], small[:, o + 10:o + 12]).then_inc(A["rden"].sem, 1)
                    own(A["rden"], g, n + 1)
                    dve.tensor_tensor(pp[:, b, :, HD:], pp[:, b, :, HD:],
                                      small[:, o + 10:o + 12].unsqueeze(2).to_broadcast([P, 2, KEYS]),
                                      ALU.mult).then_inc(A["p_ready"].sem, 1)

                def y_out(t, l):
                    n = t * LEVELS + l
                    dve.wait_ge(p_y.sem, p_y.after(g, n + 1))
                    dve.tensor_tensor(yi[:], heads(R7), per_head(cst[:, K_LEV + l, :]), ALU.mult).then_inc(y_ready.sem, 1)

                def x_out(t, l):
                    n = t * LEVELS + l
                    dve.wait_ge(p_z.sem, p_z.after(g, n + 1))
                    own(x_ready, g, t * (LEVELS + 1) + l + 1)
                    dve.tensor_tensor(xi[:], heads(R5), xi[:], ALU.add).then_inc(x_ready.sem, 1)

                for t in range(TILES):
                    tile = slice(t * P, t * P + P)
                    tok = small_tok(small)

                    def w(s, n=t + 1):
                        dve.wait_ge(s.sem, s.after(g, n))

                    scores(t, 0)
                    w(B["p_rowt"])
                    dve.tensor_copy(tok.rearrange("p (a h) -> p a h", a=2),
                                    ps[:, PT0, 0:64].rearrange("p (a h) -> p a h", a=2)[:, :, 0:4]).then_inc(B["tok"].sem, 1)
                    w(B["tok"])
                    dve.tensor_scalar(small[:, 12:16], tok[:, 4:8], -1.0, None, ALU.mult).then_inc(B["ng"].sem, 1)
                    w(B["p_gr"])
                    dve.tensor_tensor(dta[:], heads(R6), per_head(cst[:, K_CAUS, :]), ALU.add).then_inc(B["dta_r"].sem, 1)
                    dve.tensor_tensor(small[:, 24:28].unsqueeze(2), heads(R6)[:, :, P - 1:P], tok[:, 4:8].unsqueeze(2),
                                      ALU.subtract).then_inc(B["d2"].sem, 1)
                    w(B["egt"])
                    dve.scalar_tensor_tensor(out=small[:, 16:20], in0=small[:, 28:32], scalar=-1.0, in1=tok[:, 0:4],
                                             op0=ALU.mult, op1=ALU.mult).then_inc(B["c1"].sem, 1)
                    w(B["p_br"])
                    w(B["dt_r"])
                    dve.tensor_tensor(db[:], heads(R7), dt_[:], ALU.mult).then_inc(B["db_r"].sem, 1)
                    w(B["db_r"])
                    w(B["p_gg"])
                    dve.tensor_tensor(at_[:], heads(R5), db[:], ALU.mult).then_inc(B["at_r"].sem, 1)
                    w(B["at_r"])
                    dve.tensor_tensor(xi[:], at_[:], per_head(cst[:, K_M0, :]), ALU.mult).then_inc(B["x0a"].sem, 1)
                    w(B["x0a"])
                    dve.tensor_tensor(xi[:], xi[:], per_head(I), ALU.add).then_inc(x_ready.sem, 1)
                    w(B["p_kq"])
                    dve.tensor_tensor(qk[:], heads(R5), dt_[:], ALU.mult).then_inc(B["qk_r"].sem, 1)
                    w(B["p_vt"])
                    dve.tensor_tensor(vb[:], heads(PT0), wide(tok[:, 0:4]), ALU.mult).then_inc(B["vb_r"].sem, 1)
                    y_out(t, 0)
                    x_out(t, 0)
                    scores(t, 1)
                    softmax(t, 0)
                    y_out(t, 1)
                    x_out(t, 1)
                    softmax(t, 1)
                    w(B["p_kt"])
                    w(B["c1"])
                    dve.tensor_tensor(kb[:], heads(PT0 + 1), wide(small[:, 16:20]), ALU.mult).then_inc(B["kb_r"].sem, 1)
                    w(B["c2"])
                    dve.tensor_tensor(kd[:], heads(PT0 + 1), wide(small[:, 20:24]), ALU.mult).then_inc(B["kd_r"].sem, 1)
                    scores(t, 2)
                    y_out(t, 2)
                    x_out(t, 2)
                    softmax(t, 2)
                    scores(t, 3)
                    y_out(t, 3)
                    x_out(t, 3)
                    softmax(t, 3)
                    for l in (4, 5):
                        y_out(t, l)
                        x_out(t, l)
                    w(ahi)
                    dve.tensor_tensor(h_l[:, 4:8, tile], heads(OV), h_h[:, 4:8, tile].bitcast(F32),
                                      ALU.subtract).then_inc(alo.sem, 1)
                    w(B["p_su"])
                    for h in range(HEADS):
                        dve.scalar_tensor_tensor(out=state[:, h], in0=state[:, h], scalar=eg[:, h, P - 1:P],
                                                 in1=heads(R6)[:, h], op0=ALU.mult,
                                                 op1=ALU.add).then_inc(s_ready.sem, 1)
                    w(B["orr"])
                    if t:
                        w(B["mlo"], t)
                    dve.scalar_tensor_tensor(out=mx_[:], in0=heads(R5), scalar=prm[:, C_GN:C_GN + 1], in1=ro[:],
                                             op0=ALU.mult, op1=ALU.mult).then_inc(B["o1"].sem, 1)
                    w(B["o1"])
                    dve.tensor_tensor(mx_[:], mx_[:], qkvz[:, 12:16, tile], ALU.mult).then_inc(B["o2"].sem, 1)
                    w(B["mhi"])
                    dve.tensor_tensor(h_l[:, 0:4, tile], mx_[:], h_h[:, 0:4, tile].bitcast(F32),
                                      ALU.subtract).then_inc(B["mlo"].sem, 1)

                for m in range(KT):
                    split_lo(g, U_OUT, m + 1)
                    dve.wait_ge(unit_done.sem, unit_done.after(g, U_OUT + m + 1))
                    dve.tensor_tensor(xs[:, m], ps[:, m % 2, :], xs[:, m], ALU.add).then_inc(res.sem, 1)
                    if m:
                        acc_add(g, 1, m - 1)
                acc_add(g, 1, KT - 1)
                rms_apply(g, 1)
                for half in range(2):
                    with dve.Fori(0, 4) as i:
                        for s in range(4):
                            n = i * 4 + (half * 16 + s)
                            split_lo(g, i * 4 + (U_MLP + 32 * half), s + 1)
                            dve.wait_ge(fb_ready.sem, fb_ready.after(g, n + 1))
                            own(ff_ready, g, n - 1)
                            dve.tensor_tensor(ff[:, s % 2], fb[:, s % 2], fb[:, s % 2], ALU.mult).then_inc(fp_ready.sem, 1)
                            own(fp_ready, g, n + 1)
                            dve.wait_ge(fh_ready.sem, fh_ready.after(g, n + 1))
                            dve.tensor_tensor(ff_l[:, i * 4 + s, :], ff[:, s % 2], ff_h[:, i * 4 + s, :].bitcast(F32),
                                              ALU.subtract).then_inc(ff_ready.sem, 1)
                    with dve.Fori(0, 4) as i:
                        for s in range(4):
                            u = U_MLP + 16 + 32 * half
                            split_lo(g, i * 4 + u, s + 1)
                            if s % 2:
                                m = i * 2 + s // 2
                                dve.wait_ge(unit_done.sem, unit_done.after(g, i * 4 + (u + s + 1)))
                                dve.tensor_tensor(xs[:, m, :], ps[:, s // 2, :], xs[:, m, :], ALU.add).then_inc(res.sem, 1)

        @block.tensor
        def _(pe):
            def mm(o, a, b, start=True, stop=True):
                return pe.matmul(o, a, b, start=start, stop=stop)

            def unit(g, u, n, bank, rhs, start=True, stop=True, first=None):
                b = n % 2
                r_h, r_l = rhs
                pe.wait_ge(w_lo.sem, w_lo.after(g, u + (n + 1)))
                o = ps[:, bank, :]
                for k in range(KT):
                    if first:
                        first(k)
                    mm(o, w_h[:, b, k], r_h(k), start and k == 0, False)
                    mm(o, w_h[:, b, k], r_l(k), False, False)
                    last = mm(o, w_l[:, b, k], r_h(k), False, stop and k == KT - 1)
                last.then_inc(unit_done.sem, 1)

            hid = (lambda k: h_h[:, k], lambda k: h_l[:, k])

            pe.wait_ge(const_loaded, 48)
            pe.wait_ge(init_done, 2)
            pe.sem_inc(unit_done.sem, 2)
            with pe.Fori(0, GROUPS) as g:
                pe.wait_ge(acc_ready.sem, acc_ready.after(g, 8))
                mm(ps[:, OV, :], cst[:, K_MEANX, :], acc[:]).then_inc(ns_sum.sem, 1)
                pe.wait_ge(res.sem, res.after(g, 0))
                pe.wait_ge(h_ready.sem, h_ready.after(g, 8))
                pe.nop(nofuse=True)
                with pe.Fori(0, CONV // 4) as i:
                    for s in range(4):
                        pe.wait_ge(raw_ready.sem, raw_ready.after(g, (i * 4 + s) * 3 - 3))
                        unit(g, i * 4, s, s % 2, hid)
                for m in range(GATE):
                    if m < 2:
                        pe.wait_ge(raw_ready.sem, raw_ready.after(g, (CONV + m) * 3 - 3))
                    else:
                        pe.wait_ge(z_ready.sem, z_ready.after(g, m - 1))
                    unit(g, CONV, m, m % 2, hid)

                def norm_sum(n):
                    pe.wait_ge(nsq_ready.sem, nsq_ready.after(g, n + 1))
                    mm(ps[:, R5 + n % 2, :], cst[:, K_ONE if n < 8 else K_HALF, :], nq[:, n % 2]).then_inc(nsum_done.sem, 1)

                pe.wait_ge(z_ready.sem, z_ready.after(g, 3))
                unit(g, U_BA, 0, 0, hid)
                norm_sum(0)
                pe.wait_ge(z_ready.sem, z_ready.after(g, 4))
                unit(g, U_BA, 1, 1, hid)
                norm_sum(1)
                norm_sum(2)
                pe.wait_ge(row_act.sem, row_act.after(g, 2))
                unit(g, U_BA, 2, 0, hid)
                norm_sum(3)
                norm_sum(4)
                pe.wait_ge(copied.sem, copied.after(g, 1))
                for t in range(TILES):
                    last = pe.transpose(heads(OV)[:, t], avr[:, t * P:t * P + P], I)
                last.then_inc(vt_sum.sem, 1)
                for j in range(PAIRS):
                    pe.wait_ge(copied.sem, copied.after(g, j + 1))
                    unit(g, U_BA, 3 + j, (U_AQ + j) % 2, hid)
                    norm_sum(5 + 2 * j)
                    norm_sum(6 + 2 * j)

                def sc(t, j):
                    n = t * PAIRS + j
                    if n:
                        pe.wait_ge(A["ss_r"].sem, A["ss_r"].after(g, n))
                    for e in range(2):
                        r = slice(HD * e, HD * e + HD)
                        last = mm(ps[:, SC0 + e, 0:KEYS], aq[r, j, t * P:t * P + P], kn[r, t * P:t * P + KEYS])
                    last.then_inc(A["p_sc"].sem, 1)

                def pt(t, j):
                    n = t * PAIRS + j
                    pe.wait_ge(A["p_ready"].sem, A["p_ready"].after(g, n + 1))
                    o = ps[:, PT0 + j % 2, :].rearrange("p (e c k) -> p e c k", e=2, c=2)
                    for e in range(2):
                        for c in range(2):
                            last = pe.transpose(o[:, e, c], pp[:, j % 2, e, c * P:c * P + P], I)
                    last.then_inc(A["p_pt"].sem, 1)

                def ov(t, j):
                    n = t * PAIRS + j
                    pe.wait_ge(A["ptc"].sem, A["ptc"].after(g, n + 1))
                    if t == 0 and j == 0:
                        pe.wait_ge(vt_ready.sem, vt_ready.after(g, 2))
                    if t and j == 0:
                        pe.wait_ge(alo.sem, alo.after(g, t))
                    for e in range(2):
                        r = slice(HD * e, HD * e + HD)
                        for c in range(2):
                            last = mm(heads(OV)[r, j], vt[:, t + c, r], pts[:, j % 2, e, c], c == 0, c == 1)
                    if j == PAIRS - 1:
                        last.then_inc(p_ov.sem, 1)

                for t in range(TILES):
                    tile = slice(t * P, t * P + P)

                    def w(s, n=t + 1):
                        pe.wait_ge(s.sem, s.after(g, n))

                    def four(o, f, sig):
                        for h in range(HEADS):
                            last = f(o[:, h], h)
                        last.then_inc(sig.sem, 1)

                    def y_mm(l):
                        w(t_ready, t * LEVELS + l + 1)
                        four(heads(R7), lambda o, h: mm(o, at_[:, h], ti[:, h]), p_y)

                    def z_mm(l):
                        w(y_ready, t * LEVELS + l + 1)
                        four(heads(R5), lambda o, h: mm(o, yi[:, h], xi[:, h]), p_z)

                    def t_mm(l):
                        w(x_ready, t * (LEVELS + 1) + l + 1)
                        four(heads(R6), lambda o, h: pe.transpose(o, xi[:, h], I), p_t)

                    if t == 0:
                        w(normed, NORMS + 1)
                        w(row_dve, row_dve.per_group)
                    sc(t, 0)
                    pe.transpose(ps[:, PT0, 0:64], row[0:64, tile], cst[0:64, K_ID, 0:64]).then_inc(B["p_rowt"].sem, 1)
                    if t:
                        w(s_ready, t * HEADS)
                    four(heads(R6), lambda o, h: mm(o, cst[0:64, K_SEL + 4 + h, :], row[0:64, tile]), B["p_gr"])
                    if t:
                        w(B["oln"], t)
                    four(heads(R7), lambda o, h: mm(o, cst[0:64, K_SEL + h, :], row[0:64, tile]), B["p_br"])
                    if t:
                        w(B["o1"], t)
                    else:
                        w(silu_done, CONV)
                    four(heads(R5), lambda o, h: mm(o, qkvz[:, 4 + h, tile], qkvz[:, 4 + h, tile]), B["p_gg"])
                    four(heads(PT0 + 1), lambda o, h: pe.transpose(o, qkvz[:, 4 + h, tile], I), B["p_kt"])
                    w(B["tok"])
                    four(heads(PT0), lambda o, h: pe.transpose(o, qkvz[:, 8 + h, tile], I), B["p_vt"])
                    w(B["at_r"])
                    four(heads(R5), lambda o, h: mm(o, qkvz[:, 4 + h, tile], qkvz[:, h, tile]), B["p_kq"])
                    w(B["eg_r"])
                    t_mm(0)
                    y_mm(0)
                    sc(t, 1)
                    w(B["qk_r"])
                    z_mm(0)
                    t_mm(1)
                    w(B["vb_r"])
                    y_mm(1)
                    pt(t, 0)
                    z_mm(1)
                    sc(t, 2)
                    t_mm(2)
                    ov(t, 0)
                    w(B["kd_r"])
                    y_mm(2)
                    pt(t, 1)
                    z_mm(2)
                    sc(t, 3)
                    t_mm(3)
                    ov(t, 1)
                    y_mm(3)
                    pt(t, 2)
                    z_mm(3)
                    t_mm(4)
                    ov(t, 2)
                    y_mm(4)
                    pt(t, 3)
                    z_mm(4)
                    t_mm(5)
                    ov(t, 3)
                    y_mm(5)
                    z_mm(5)
                    w(x_ready, (t + 1) * (LEVELS + 1))
                    four(heads(R6), lambda o, h: mm(o, kb[:, h], xi[:, h]), B["p_wt"])
                    w(B["wtc"])
                    for h in range(HEADS):
                        mm(heads(R7)[:, h], xi[:, h], vb[:, h], True, False)
                        last = mm(heads(R7)[:, h], wt[:, h], state[:, h], False, True)
                    last.then_inc(B["p_vv"].sem, 1)
                    w(B["qd_r"])
                    w(B["vnc"])
                    for h in range(HEADS):
                        mm(heads(R5)[:, h], state[:, h], qd[:, h], True, False)
                        last = mm(heads(R5)[:, h], vn[:, h], qk[:, h], False, True)
                    last.then_inc(B["p_oo"].sem, 1)
                    four(heads(R6), lambda o, h: mm(o, kd[:, h], vn[:, h]), B["p_su"])
                    w(B["osq_r"])
                    last = mm(ps[:, R7, :], cst[:, K_MEAN, :], osq[:].rearrange("p h c -> p (h c)"))
                    last.then_inc(B["p_on"].sem, 1)

                last = pe.transpose(ps[:, SC0, 0:P], I, I)
                last.then_inc(unit_done.sem, 1)
                pe.wait_ge(B["mlo"].sem, B["mlo"].after(g, TILES))
                pe.wait_ge(alo.sem, alo.after(g, TILES))
                for m in range(KT):
                    if m >= 2:
                        pe.wait_ge(res.sem, res.after(g, m - 1))
                    unit(g, U_OUT, m, m % 2, hid)
                pe.wait_ge(acc_ready.sem, acc_ready.after(g, 16))
                mm(ps[:, OV, :], cst[:, K_MEANX, :], acc[:]).then_inc(ns_sum.sem, 1)
                pe.wait_ge(h_ready.sem, h_ready.after(g, 16))
                for half in range(2):
                    if half == 0:
                        pe.wait_ge(res.sem, res.after(g, KT))
                    else:
                        pe.wait_ge(res.sem, res.after(g, 2 * KT))
                    pe.nop(nofuse=True)
                    with pe.Fori(0, 4) as i:
                        for s in range(4):
                            pe.wait_ge(fp_ready.sem, fp_ready.after(g, i * 4 + (16 * half + s - 1)))
                            unit(g, i * 4 + (U_MLP + 32 * half), s, s % 2, hid)
                    pe.wait_ge(fb_ready.sem, fb_ready.after(g, 16 * half + 16))
                    pe.nop(nofuse=True)
                    with pe.Fori(0, 4) as i:
                        for s in range(4):
                            kq = s % 2
                            if s % 2 == 0:
                                pe.wait_ge(res.sem, res.after(g, i * 2 + (KT + KT * half + s // 2 - 1)))
                            pe.wait_ge(ff_ready.sem, ff_ready.after(g, 16 * half + 8 * kq + 8))
                            hidden = (lambda k: ff_h[:, 8 * kq + k], lambda k: ff_l[:, 8 * kq + k])
                            unit(g, i * 4 + (U_MLP + 16 + 32 * half), s, s // 2, hidden, kq == 0, kq == 1)


def small_tok(small):
    return small[:, 44:52]


def convw(prm, m, j):
    return prm[:, C_CONV:C_CONV + 4 * CONV].rearrange("p (m j) -> p m j", j=4)[:, m, j:j + 1]


def u_div(u, n):
    return u // SLOTS + n // SLOTS



def constants():
    i = np.arange(P)
    c = np.zeros((P, N_CONST, P), np.float32)
    c[:, K_ID] = np.eye(P)
    c[:, K_ONE] = 1.0
    c[:, K_MEAN] = 1.0 / P
    c[:, K_MEANX] = 1.0 / D
    c[:, K_HALF] = (i[:, None] // HD == i[None, :] // HD) / HD
    c[:, K_CAUS] = np.where(i[:, None] <= i[None, :], 0.0, NEG)
    c[:, K_M0] = -1.0 * ((i[:, None] % 2 == 0) & (i[None, :] == i[:, None] + 1))
    for l in range(LEVELS):
        b = 2 << l
        c[:, K_LEV + l] = -1.0 * ((i[:, None] // (2 * b) == i[None, :] // (2 * b))
                                  & (i[:, None] % (2 * b) >= b) & (i[None, :] % (2 * b) < b))
    for h in range(HEADS):
        c[h, K_SEL + h] = 1.0
        c[32 + h, K_SEL + 4 + h] = 1.0
    q, k = i[:, None], np.arange(KEYS)[None, :]
    dist = np.abs(q + HD - k).astype(np.float32)
    seen = np.where(q < HD, k < 2 * HD, k >= HD)
    b = np.zeros((P, 2, PAIRS, 2, KEYS), np.float32)
    for j in range(PAIRS):
        for e in range(2):
            slope = np.float32(2.0 ** -(4 * e + j + 1))
            b[:, 0, j, e] = np.where(seen & (k >= HD), -slope * dist, NEG)
            b[:, 1, j, e] = np.where(seen, -slope * dist, NEG)
    return c.reshape(P, -1), b.reshape(P, -1)


def weight_units(w_in, w_out, w1, w2):
    def tile(m):
        return m.reshape(KT, P, P).transpose(1, 0, 2).reshape(P, KT * P)

    u = np.zeros((UNITS, P, KT * P), np.float32)
    for m in range(16):
        u[m] = tile(w_in[:, m * P:m * P + P])
    ba = np.zeros((D, P), np.float32)
    ba[:, 0:4] = w_in[:, 2048:2052]
    ba[:, 32:36] = w_in[:, 2052:2056]
    u[U_BA] = tile(ba)
    q0, k0, v0 = 2056, 2568, 2696
    for j in range(PAIRS):
        cols = [q0 + HD * h + c for h in (j, 4 + j) for c in range(HD)]
        u[U_AQ + j] = tile(w_in[:, cols])
    u[U_AK] = tile(w_in[:, k0:k0 + P])
    u[U_AV] = tile(w_in[:, v0:v0 + P])
    rows = list(range(512)) + [512 + HD * h + c for j in range(PAIRS) for h in (j, 4 + j) for c in range(HD)]
    wo = w_out[rows]
    for m in range(KT):
        cols = slice(m * P, m * P + P)
        u[U_OUT + m] = tile(wo[:, cols])
        for half in range(2):
            for kq in range(2):
                r = half * 2048 + kq * 1024
                u[U_MLP + 16 + 32 * half + 2 * m + kq] = tile(w2[r:r + 1024, cols])
    for m in range(32):
        u[U_MLP + 32 * (m // 16) + m % 16] = tile(w1[:, m * P:m * P + P])
    return u


def parameters(norm1_w, norm2_w, conv_w, gdn_norm_w, q_norm_w, k_norm_w, a_log, dt_bias, sinks):
    p = np.zeros((P, N_PAR), np.float32)
    p[:, C_N1:C_N1 + 8] = norm1_w[0].reshape(8, P).T
    p[:, C_N2:C_N2 + 8] = norm2_w[0].reshape(8, P).T
    p[:, C_CONV:C_CONV + 48] = conv_w[0].reshape(4, CONV, P).transpose(2, 1, 0).reshape(P, 48)
    p[:, C_GN] = gdn_norm_w[0]
    p[:, C_QN] = np.concatenate([q_norm_w[0]] * 2)
    p[:, C_KN] = np.concatenate([k_norm_w[0]] * 2)
    p[32:36, C_ALOG] = a_log[0]
    p[32:36, C_DT] = dt_bias[0]
    p[:, C_SINK:] = sinks[0].reshape(2, PAIRS).T.reshape(-1)[None, :]
    return p


def kernel(x, norm1_w, w_in, conv_w, a_log, dt_bias, gdn_norm_w, q_norm_w, k_norm_w, sinks, w_out, norm2_w, w1, w2):
    import concourse.bacc as bacc
    from concourse.bass_utils import run_bass_kernel_spmd

    (x, norm1_w, w_in, conv_w, a_log, dt_bias, gdn_norm_w, q_norm_w, k_norm_w, sinks, w_out, norm2_w, w1, w2) = (
        np.asarray(a) for a in (x, norm1_w, w_in, conv_w, a_log, dt_bias, gdn_norm_w, q_norm_w, k_norm_w, sinks,
                                w_out, norm2_w, w1, w2))
    con, bias = constants()
    arrays = {
        "x": np.ascontiguousarray(x[0].reshape(GROUPS, TOK, KT, P).transpose(0, 3, 2, 1)),
        "w": weight_units(w_in[0], w_out[0], w1[0], w2[0]),
        "par": parameters(norm1_w, norm2_w, conv_w, gdn_norm_w, q_norm_w, k_norm_w, a_log, dt_bias, sinks),
        "con": con.reshape(P, N_CONST, P),
        "bias": bias,
    }
    nc = bacc.Bacc("TRN2", target_bir_lowering=False, num_devices=1)
    ins = [nc.dram_tensor(n, a.shape, F32, kind="ExternalInput").ap() for n, a in arrays.items()]
    out = nc.dram_tensor("out", (GROUPS, P, KT, TOK), F32, kind="ExternalOutput").ap()
    build(nc, *ins, out)
    y = run_bass_kernel_spmd(nc, [arrays], core_ids=[0]).results[0]["out"]
    return np.ascontiguousarray(y.transpose(0, 3, 2, 1)).reshape(1, SEQ, D)
```

```python
import math

from contextlib import ExitStack

import numpy as np

import concourse.bass as bass
from concourse import mybir

F32 = mybir.dt.float32
F32R = mybir.dt.float32r
ALU = mybir.AluOpType
ACT = mybir.ActivationFunctionType
AX = mybir.AxisListType

P = 128
D = 1024
SEQ = 2048
TOK = 512
GROUPS = SEQ // TOK
TILES = TOK // P
KT = D // P
HEADS = 4
PAIRS = 4
HD = 64
KEYS = 192
LEVELS = 6
EPS = 1e-6
NEG = -1e30

CONV, GATE = 12, 4
U_BA, U_AV, U_AK, U_AQ = 16, 17, 18, 19
U_PAD, U_OUT, U_MLP = 23, 24, 32
UNITS = 96
NORMS = 13
SLOTS = 4
XPARTS = 4

C_N1, C_N2, C_CONV, C_GN, C_QN, C_KN, C_ALOG, C_DT, C_SINK = 0, 8, 16, 64, 65, 66, 67, 68, 69
N_PAR = C_SINK + 2 * PAIRS
K_ID, K_ONE, K_MEAN, K_MEANX, K_HALF, K_CAUS, K_M0, K_LEV, K_SEL = 0, 1, 2, 3, 4, 5, 6, 7, 10
N_CONST = K_SEL + 2 * HEADS


class Signal:

    def __init__(self, sem, per_group, credit=0, step=1):
        self.sem, self.per_group, self.credit, self.step = sem, per_group, credit, step

    def after(self, g, n):
        return g * (self.per_group * self.step) + n * self.step + self.credit


def build(nc, x, w, par, con, bias, out):
    with ExitStack() as ctx:
        def sb(name, shape, dt=F32, scope=ctx):
            return scope.enter_context(nc.sbuf_tensor(name, shape, dt))

        def signal(name, per_group, credit=0, step=1):
            return Signal(ctx.enter_context(nc.semaphore(name)), per_group, credit, step)

        stage = sb("stage", [P, SLOTS, KT, P])
        w_h = sb("w_h", [P, 2, KT, P], F32R)
        w_l = sb("w_l", [P, 2, KT, P], F32R)
        xs = sb("xs", [P, KT, TOK])
        h_h = sb("h_h", [P, KT, TOK], F32R)
        with ExitStack() as s:
            x_next = sb("x_next", [P, KT, TOK], F32, s)
        h_l = sb("h_l", [P, KT, TOK], F32R)
        aq = sb("aq", [P, PAIRS, TOK])
        kn = sb("kn", [P, HD + TOK])
        vt = sb("vt", [P, 1 + TILES, P])
        state = sb("state", [P, HEADS, P])
        tail = sb("tail", [P, CONV, 3])
        row = sb("row", [64, TOK])
        cst = sb("cst", [P, N_CONST, P])
        bia = sb("bia", [P, 2, PAIRS, 2, KEYS])
        prm = sb("prm", [P, N_PAR])
        nalog = sb("nalog", [P, 1])
        nsink = sb("nsink", [P, 2 * PAIRS])
        eps = sb("eps", [P, 1])
        att = sb("att", [P, 2, 12])
        sm = sb("sm", [P, TILES, 28])
        with ExitStack() as s:
            ff_h = sb("ff_h", [P, 16, TOK], F32R, s)
            ff_l = sb("ff_l", [P, 16, TOK], F32R, s)
        qkvz = sb("qkvz", [P, 16, TOK])
        with ExitStack() as s:
            raw = sb("raw", [P, 2, 3 + TOK], F32, s)
            cy = sb("cy", [P, 2, TOK], F32, s)
            nq = sb("nq", [P, 2, TOK], F32, s)
            rr = sb("rr", [P, 2, TOK], F32, s)
            akr = sb("akr", [P, TOK], F32, s)
            avr = sb("avr", [P, TOK], F32, s)
            rw = sb("rw", [P, 4, TOK], F32, s)
        eg = sb("eg", [P, 2, HEADS, P])
        d1 = sb("d1", [P, 2, HEADS, P])
        dt_ = sb("dt", [P, 2, HEADS, P])
        at_ = sb("at", [P, 2, HEADS, P])
        xi = sb("xi", [P, 2, HEADS, P])
        ti = sb("ti", [P, 2, HEADS, P])
        kb = sb("kb", [P, 2, HEADS, P])
        qk = sb("qk", [P, 2, HEADS, P])
        with ExitStack() as s:
            sq = sb("sq", [P, 2, TOK], F32, s)
            acc = sb("acc", [P, TOK], F32, s)
            rt = sb("rt", [P, TOK], F32, s)
            ht = sb("ht", [P, 2, TOK], F32, s)
            fb = sb("fb", [P, 2, TOK], F32, s)
            ff = sb("ff", [P, 2, TOK], F32, s)
        ss = sb("ss", [P, 2, 2, KEYS])
        pp = sb("pp", [P, 2, 2, 256])
        pts = sb("pts", [P, 2, 2, 2, P])

        ps = ctx.enter_context(nc.psum_tensor("ps", [P, 8, 512], F32))
        SC0, PT, OV, NS, A0 = 0, 2, 3, 4, 6

        def ring(a, k):
            return 4 + 2 * a + k % 2

        def heads(b):
            return ps[:, b, :].rearrange("p (h c) -> p h c", h=HEADS)

        I = cst[:, K_ID, :]
        R64, A4 = slice(0, 64), slice(32, 36)
        X, E, U, L = (rw[R64, i] for i in range(4))

        def wide(v):
            return v.unsqueeze(2).to_broadcast([P, HEADS, P])

        BETA, GC, NGC, DGC, EGC, CB, CD = (slice(4 * i, 4 * i + 4) for i in range(7))
        MAX, NMAX, SUM, SDIF, SEXP, RDEN = (slice(2 * i, 2 * i + 2) for i in range(6))

        def first_half(m, l):
            return m.rearrange("p (n two b) -> p n two b", two=2, b=2 << l)[:, :, 0, :]

        def flat(m):
            return m.rearrange("p h c -> p (h c)")

        def per_head(m):
            return m.unsqueeze(1).to_broadcast([P, HEADS, P])

        par_loaded = ctx.enter_context(nc.semaphore("par_loaded"))
        const_loaded = ctx.enter_context(nc.semaphore("const_loaded"))
        bias_loaded = ctx.enter_context(nc.semaphore("bias_loaded"))
        init_done = ctx.enter_context(nc.semaphore("init_done"))
        init_act = ctx.enter_context(nc.semaphore("init_act"))
        w_loaded = [signal(f"w_loaded{i}", UNITS // SLOTS, step=16) for i in range(SLOTS)]
        w_hi = signal("w_hi", UNITS)
        w_lo = signal("w_lo", UNITS, credit=SLOTS)
        unit_done = signal("unit_done", UNITS, credit=2)
        x_loaded = signal("x_loaded", 1, step=16)
        next_loaded = [signal(f"next_loaded{i}", 1, step=16) for i in range(XPARTS)]
        y_stored = signal("y_stored", KT, step=16)
        N1, N2 = ({n: signal(f"{n}{i}", c) for n, c in
                   (("sq_ready", KT), ("acc_ready", KT), ("mean_done", 1), ("rt_ln", 1), ("rt_ready", 1),
                    ("hh_ready", KT), ("h_ready", KT))} for i in (1, 2))
        ht_ready = signal("ht_ready", KT)
        raw_ready = signal("raw_ready", 3 * CONV, credit=6)
        tap_done = signal("tap_done", 4 * CONV)
        silu_done = signal("silu_done", CONV, credit=2)
        z_ready = signal("z_ready", GATE)
        copied = signal("copied", 6)
        nsq_ready = signal("nsq_ready", NORMS)
        nsum_done = signal("nsum_done", NORMS)
        nln_done = signal("nln_done", NORMS)
        nrr_ready = signal("nrr_ready", NORMS)
        normed = signal("normed", NORMS + 1)
        row_act = signal("row_act", 5)
        row_dve = signal("row_dve", 8 + TILES)
        vt_sum = signal("vt_sum", 1)
        vt_ready = signal("vt_ready", 2)
        B = {n: signal(n, TILES) for n in
             ("p_gr p_br p_gg p_kt p_vt p_kq p_t0 p_wt p_vv p_oo p_su p_on "
              "dta_r d2 db_r at_r x0a x0 qk_r vb_r kb_r kd_r o1 o2 mlo "
              "eg_r dt_r t0 wtc vnc osq_r oln orr mhi qd_r").split()}
        B2 = {n: signal(n, 2) for n in ("c2",)}
        B1 = {n: signal(n, 1) for n in "p_rowt tok ng c1 egt".split()}
        p_y = signal("p_y", TILES * LEVELS)
        p_u = signal("p_u", TILES * LEVELS)
        p_x = signal("p_x", TILES * LEVELS)
        y_ready = signal("y_ready", TILES * LEVELS)
        t_ready = signal("t_ready", TILES * LEVELS)
        x_ready = signal("x_ready", TILES * LEVELS)
        s_ready = signal("s_ready", TILES * HEADS)
        A = {n: signal(n, TILES * PAIRS) for n in
             "p_sc p_pt ss_r amax nmax sdiff den_r rden p_ready es_r ptc".split()}
        p_ov = signal("p_ov", TILES)
        ahi = signal("ahi", TILES)
        alo = signal("alo", TILES)
        pads = signal("pads", 1)
        res = signal("res", KT + 2 * KT, credit=1)
        fb_ready = signal("fb_ready", 32, credit=2)
        fh_ready = signal("fh_ready", 32)
        fp_ready = signal("fp_ready", 32)
        ff_ready = signal("ff_ready", 32, credit=2)

        block = ctx.enter_context(nc.Block())

        @block.sync
        def _(sp):
            def load(u, s, dst_wait=None):
                sp.dma_start(stage[:, s], w[u].rearrange("p (k m) -> p k m", k=KT)).then_inc(w_loaded[s].sem, 16)

            sp.dma_start(prm[:], par).then_inc(par_loaded, 16)
            sp.dma_start(cst[:], con).then_inc(const_loaded, 16)
            with sp.Fori(0, GROUPS) as g:
                with sp.Fori(0, UNITS // SLOTS) as i:
                    for s in range(SLOTS):
                        sp.wait_ge(w_lo.sem, w_lo.after(g, i * SLOTS + (s + 1 - SLOTS)))
                        load(i * SLOTS + s, s)
            sp.wait_ge(w_lo.sem, w_lo.after(GROUPS, 1 - SLOTS))
            load(0, 0)

        @block.gpsimd
        def _(pool):
            def load_next(g):
                for i in range(XPARTS):
                    part = slice(i * (KT // XPARTS), (i + 1) * (KT // XPARTS))
                    pool.dma_start(x_next[:, part], x[g, :, part]).then_inc(next_loaded[i].sem, 16)

            load_next(0)
            pool.dma_start(bia[:], bias.rearrange("p (v j e k) -> p v j e k", v=2, j=PAIRS, e=2)).then_inc(bias_loaded, 16)
            with pool.Fori(0, GROUPS) as g:
                pool.dma_start(xs[:], x[g]).then_inc(x_loaded.sem, 16)
                for t in range(TILES):
                    q_tile = qkvz[:, 0:4, t * P:t * P + P]
                    pool.wait_ge(B["p_kq"].sem, B["p_kq"].after(g, t + 1))
                    pool.wait_ge(B["eg_r"].sem, B["eg_r"].after(g, t + 1))
                    nc.gpsimd.tensor_tensor(q_tile, q_tile, eg[:, t % 2], ALU.mult).then_inc(B["qd_r"].sem, 1)
                pool.wait_ge(unit_done.sem, unit_done.after(g, U_MLP + 32 + 16))
                pool.nop(nofuse=True)
                load_next((g + 1) % GROUPS)
                for m in range(KT):
                    pool.wait_ge(res.sem, res.after(g, 2 * KT + m + 1))
                    pool.nop(nofuse=True)
                    pool.dma_start(out[g, :, m], xs[:, m]).then_inc(y_stored.sem, 16)
                pool.wait_ge(y_stored.sem, y_stored.after(g, KT))
                pool.nop(nofuse=True)
            pool.wait_ge(x_loaded.sem, x_loaded.after(GROUPS, 0))
            for part in next_loaded:
                pool.wait_ge(part.sem, part.after(GROUPS, 1))

        @block.scalar
        def _(act):
            def split_hi(g, u, n=0):
                s, b = n % SLOTS, n % 2
                act.wait_ge(w_loaded[s].sem, w_loaded[s].after(g, u_div(u, n) + 1))
                act.wait_ge(unit_done.sem, unit_done.after(g, u + (n - 1)))
                act.copy(w_h[:, b], stage[:, s]).then_inc(w_hi.sem, 1)

            def square(N, g, k, src):
                if k >= 2:
                    act.wait_ge(N["acc_ready"].sem, N["acc_ready"].after(g, k - 1))
                act.activation(sq[:, k % 2], src, ACT.Square).then_inc(N["sq_ready"].sem, 1)

            def root(N, g):
                act.wait_ge(N["mean_done"].sem, N["mean_done"].after(g, 1))
                act.activation(rt[:], ps[:, OV, :], ACT.Ln, bias=eps[:, 0:1]).then_inc(N["rt_ln"].sem, 1)
                act.wait_ge(N["rt_ln"].sem, N["rt_ln"].after(g, 1))
                act.activation(rt[:], rt[:], ACT.Exp, scale=-0.5).then_inc(N["rt_ready"].sem, 1)

            def n1_square(g, k):
                part = next_loaded[k // (KT // XPARTS)]
                act.wait_ge(part.sem, part.after(g, 1))
                square(N1, g, k, x_next[:, k])

            def n1_high(g, k):
                act.wait_ge(ht_ready.sem, ht_ready.after(g, k + 1))
                act.copy(h_h[:, k], ht[:, k % 2]).then_inc(N1["hh_ready"].sem, 1)

            act.wait_ge(par_loaded, 16)
            act.wait_ge(init_done, 1)
            act.preload_act_table_set("natural_log_exp_and_others")
            act.activation(nalog[32:36], prm[32:36, C_ALOG:C_ALOG + 1], ACT.Exp).then_inc(init_act, 1)
            act.sem_inc(raw_ready.sem, 6)
            act.sem_inc(silu_done.sem, 2)
            split_hi(0, 0)
            for k in range(KT):
                n1_square(0, k)
            root(N1, 0)
            for k in range(KT):
                n1_high(0, k)

            with act.Fori(0, GROUPS) as g:
                act.preload_act_table_set("silu_and_others")

                def silu(m, s):
                    act.wait_ge(tap_done.sem, tap_done.after(g, m * 4 + 4))
                    act.activation(qkvz[:, m, :], cy[:, s % 2], ACT.Silu).then_inc(silu_done.sem, 1)

                def conv_input(i, s):
                    split_hi(g, i * 4, s + 1)
                    act.wait_ge(unit_done.sem, unit_done.after(g, i * 4 + s + 1))
                    act.copy(raw[:, s % 2, 3:], ps[:, A0 + s % 2, :]).then_inc(raw_ready.sem, 1)
                    act.copy(raw[:, s % 2, 0:3], tail[:, i * 4 + s, :]).then_inc(raw_ready.sem, 1)
                    act.wait_ge(raw_ready.sem, raw_ready.after(g, (i * 4 + s) * 3 + 2))
                    act.nop(nofuse=True)
                    act.copy(tail[:, i * 4 + s, :], ps[:, A0 + s % 2, TOK - 3:]).then_inc(raw_ready.sem, 1)

                for s in range(4):
                    conv_input(0, s)
                    if s:
                        silu(s - 1, s - 1)
                with act.Fori(1, CONV // 4) as i:
                    for s in range(4):
                        conv_input(i, s)
                        silu(i * 4 + (s - 1), s - 1)
                for m in range(GATE):
                    split_hi(g, CONV, m + 1)
                    if m == 0:
                        silu(CONV - 1, CONV - 1)
                    act.wait_ge(unit_done.sem, unit_done.after(g, CONV + m + 1))
                    act.activation(qkvz[:, 12 + m, :], ps[:, A0 + m % 2, :], ACT.Silu).then_inc(z_ready.sem, 1)

                act.preload_act_table_set("natural_log_exp_and_others")

                def norm_root(n):
                    act.wait_ge(nsum_done.sem, nsum_done.after(g, n + 1))
                    act.activation(rr[:, n % 2], ps[:, NS + n % 2, :], ACT.Ln, bias=eps[:, 0:1]).then_inc(nln_done.sem, 1)
                    act.wait_ge(nln_done.sem, nln_done.after(g, n + 1))
                    act.activation(rr[:, n % 2], rr[:, n % 2], ACT.Exp, scale=-0.5).then_inc(nrr_ready.sem, 1)

                split_hi(g, U_BA, 1)
                act.wait_ge(unit_done.sem, unit_done.after(g, U_BA + 1))
                act.activation(X, ps[R64, A0, :], ACT.Identity, bias=prm[R64, C_DT:C_DT + 1]).then_inc(row_act.sem, 1)
                act.copy(rw[0:32, 1], ps[0:32, A0, :]).then_inc(row_act.sem, 1)
                norm_root(0)
                split_hi(g, U_BA, 2)
                act.wait_ge(unit_done.sem, unit_done.after(g, U_AV + 1))
                act.copy(avr[:], ps[:, A0 + 1, :]).then_inc(copied.sem, 1)
                act.wait_ge(row_dve.sem, row_dve.after(g, 1))
                act.wait_ge(row_act.sem, row_act.after(g, 2))
                act.activation(E, E, ACT.Exp, scale=-1.0).then_inc(row_act.sem, 1)
                norm_root(1)
                norm_root(2)
                split_hi(g, U_BA, 3)
                act.wait_ge(unit_done.sem, unit_done.after(g, U_AK + 1))
                act.copy(akr[:], ps[:, A0, :]).then_inc(copied.sem, 1)
                act.wait_ge(row_dve.sem, row_dve.after(g, 2))
                act.activation(L, U, ACT.Ln).then_inc(row_act.sem, 1)
                norm_root(3)
                norm_root(4)
                act.copy(vt[:, 0], vt[:, TILES]).then_inc(vt_ready.sem, 1)
                act.wait_ge(vt_ready.sem, vt_ready.after(g, 1))
                act.wait_ge(vt_sum.sem, vt_sum.after(g, 1))
                act.copy(vt[:, 1:], heads(OV)).then_inc(vt_ready.sem, 1)
                for j in range(PAIRS):
                    split_hi(g, U_BA, 4 + j)
                    act.wait_ge(unit_done.sem, unit_done.after(g, U_AQ + j + 1))
                    act.copy(aq[:, j], ps[:, A0 + (U_AQ + j) % 2, :]).then_inc(copied.sem, 1)
                    if j == 0:
                        act.wait_ge(row_dve.sem, row_dve.after(g, 3))
                        act.wait_ge(row_act.sem, row_act.after(g, 4))
                        act.activation(U, L, ACT.Exp, scale=-1.0).then_inc(row_act.sem, 1)
                    norm_root(5 + 2 * j)
                    norm_root(6 + 2 * j)
                split_hi(g, U_BA, 8)

                def exps(n):
                    b = n % 2
                    act.wait_ge(A["nmax"].sem, A["nmax"].after(g, n + 1))
                    if n == 0:
                        act.wait_ge(pads.sem, pads.after(g, 1))
                    for e in range(2):
                        act.activation(pp[:, b, e, HD:], ss[:, b, e], ACT.Exp, bias=att[:, b, NMAX][:, e:e + 1],
                                       accum_out=att[:, b, SUM][:, e:e + 1])
                    act.wait_ge(A["sdiff"].sem, A["sdiff"].after(g, n + 1))
                    act.activation(att[:, b, SEXP], att[:, b, SDIF], ACT.Exp).then_inc(A["es_r"].sem, 1)

                def pt_copy(n):
                    act.wait_ge(A["p_pt"].sem, A["p_pt"].after(g, n + 1))
                    act.copy(pts[:, n % 2], ps[:, PT, :].rearrange("p (e c k) -> p e c k", e=2, c=2)).then_inc(A["ptc"].sem, 1)

                for q in range(TILES // 2):
                    def tick(k):
                        if 0 <= k - 2 < 2 * PAIRS:
                            pt_copy(q * 2 * PAIRS + k - 2)
                        if k < 2 * PAIRS:
                            exps(q * 2 * PAIRS + k)

                    def att_out(a):
                        t = 2 * q + a
                        act.wait_ge(p_ov.sem, p_ov.after(g, t + 1))
                        act.copy(h_h[:, 4:8, t * P:t * P + P], heads(OV)).then_inc(ahi.sem, 1)

                    def w(s, a):
                        act.wait_ge(s.sem, s.after(g, 2 * q + a + 1))

                    if q == 0:
                        act.wait_ge(B1["tok"].sem, B1["tok"].after(g, 1))
                        act.activation(sm[:, :, EGC], sm[:, :, GC], ACT.Exp).then_inc(B1["egt"].sem, 1)
                        act.wait_ge(B1["ng"].sem, B1["ng"].after(g, 1))
                    for a in range(2):
                        w(B["d2"], a)
                        act.activation(eg[:, a], heads(ring(a, 0)), ACT.Exp).then_inc(B["eg_r"].sem, 1)
                        for h in range(HEADS):
                            e = act.activation(dt_[:, a, h], d1[:, a, h], ACT.Exp, bias=sm[:, 2 * q + a, NGC][:, h:h + 1])
                        e.then_inc(B["dt_r"].sem, 1)
                    tick(0)
                    pair = slice(2 * q, 2 * q + 2)
                    act.activation(sm[:, pair, CD], sm[:, pair, DGC], ACT.Exp).then_inc(B2["c2"].sem, 1)
                    for a in range(2):
                        w(B["p_t0"], a)
                        act.copy(ti[:, a], heads(ring(a, 0))).then_inc(B["t0"].sem, 1)
                    tick(1)
                    for l in range(LEVELS + 1):
                        for a in range(2):
                            if l:
                                n = q * 2 * LEVELS + 2 * (l - 1) + a
                                act.wait_ge(p_x.sem, p_x.after(g, n + 1))
                                act.copy(xi[:, a], heads(ring(a, 3 * l + 1))).then_inc(x_ready.sem, 1)
                        for k in (2 + 2 * l, 3 + 2 * l):
                            if k <= 10:
                                tick(k)
                            if k in (6, 10):
                                att_out(k // 10)
                    for a in range(2):
                        w(B["p_wt"], a)
                        act.copy(ti[:, a], heads(ring(a, 0))).then_inc(B["wtc"].sem, 1)

                    def v_new(a):
                        w(B["p_vv"], a)
                        act.copy(d1[:, a], heads(ring(a, 1))).then_inc(B["vnc"].sem, 1)

                    def out_square(a):
                        w(B["p_oo"], a)
                        act.activation(at_[:, a], heads(ring(a, 0)), ACT.Square).then_inc(B["osq_r"].sem, 1)

                    def out_root(a):
                        w(B["p_on"], a)
                        act.activation(dt_[:, a], heads(PT), ACT.Ln, bias=eps[:, 0:1]).then_inc(B["oln"].sem, 1)
                        w(B["oln"], a)
                        act.activation(dt_[:, a], dt_[:, a], ACT.Exp, scale=-0.5).then_inc(B["orr"].sem, 1)

                    def mix_hi(a):
                        t = 2 * q + a
                        w(B["o2"], a)
                        act.copy(h_h[:, 0:4, t * P:t * P + P], eg[:, a]).then_inc(B["mhi"].sem, 1)

                    v_new(0)
                    out_square(0)
                    v_new(1)
                    out_root(0)
                    out_square(1)
                    mix_hi(0)
                    out_root(1)
                    mix_hi(1)

                for m in range(KT + 1):
                    if m < KT:
                        split_hi(g, U_OUT, m + 1)
                    if m:
                        act.wait_ge(res.sem, res.after(g, m))
                        if m < KT:
                            square(N2, g, m - 1, xs[:, m - 1])
                act.wait_ge(unit_done.sem, unit_done.after(g, U_OUT + KT))
                for k in range(KT):
                    act.activation(h_h[:, k], xs[:, k], ACT.Copy, scale=prm[:, C_N2 + k:C_N2 + k + 1]).then_inc(N2["hh_ready"].sem, 1)
                    if k == 1:
                        square(N2, g, KT - 1, xs[:, KT - 1])

                def up(half, i, s, first=False):
                    n = i * 4 + (half * 16 + s)
                    split_hi(g, i * 4 + (U_MLP + 32 * half), s + 1)
                    if first:
                        root(N2, g)
                    act.wait_ge(fb_ready.sem, fb_ready.after(g, n + 1))
                    act.activation(ff_h[:, i * 4 + s, :], fb[:, s % 2], ACT.Square).then_inc(fh_ready.sem, 1)

                for s in range(4):
                    up(0, 0, s, s == 0)
                with act.Fori(1, 4) as i:
                    for s in range(4):
                        up(0, i, s)
                with act.Fori(0, 4) as i:
                    for s in range(4):
                        split_hi(g, i * 4 + (U_MLP + 16), s + 1)
                with act.Fori(0, 4) as i:
                    for s in range(4):
                        up(1, i, s)
                for s in range(16):
                    split_hi(g, U_MLP + 48, s + 1)
                    if 4 <= s < 8:
                        n1_square(g + 1, 2 * s - 8)
                        n1_square(g + 1, 2 * s - 7)
                    if s == 8:
                        root(N1, g + 1)
                    if 10 <= s < 14:
                        n1_high(g + 1, 2 * s - 20)
                        n1_high(g + 1, 2 * s - 19)

        @block.vector
        def _(dve):
            def own(sig, g, n):
                dve.wait_ge(sig.sem, sig.after(g, n))

            def split_lo(g, u, n=0):
                s, b = n % SLOTS, n % 2
                dve.wait_ge(w_hi.sem, w_hi.after(g, u + (n + 1)))
                dve.tensor_tensor(w_l[:, b], stage[:, s], w_h[:, b].bitcast(F32), ALU.subtract).then_inc(w_lo.sem, 1)

            def acc_add(N, g, k):
                dve.wait_ge(N["sq_ready"].sem, N["sq_ready"].after(g, k + 1))
                if k == 0:
                    dve.tensor_copy(acc[:], sq[:, 0]).then_inc(N["acc_ready"].sem, 1)
                else:
                    own(N["acc_ready"], g, k)
                    dve.tensor_tensor(acc[:], acc[:], sq[:, k % 2], ALU.add).then_inc(N["acc_ready"].sem, 1)

            def n1_norm(g, k):
                if k >= 2:
                    own(N1["h_ready"], g, k - 1)
                dve.scalar_tensor_tensor(out=ht[:, k % 2], in0=x_next[:, k], scalar=prm[:, C_N1 + k:C_N1 + k + 1],
                                         in1=rt[:], op0=ALU.mult, op1=ALU.mult).then_inc(ht_ready.sem, 1)

            def n1_low(g, k):
                dve.wait_ge(N1["hh_ready"].sem, N1["hh_ready"].after(g, k + 1))
                dve.tensor_tensor(h_l[:, k], ht[:, k % 2], h_h[:, k].bitcast(F32), ALU.subtract).then_inc(N1["h_ready"].sem, 1)

            dve.memset(eps[:], EPS).then_inc(init_done, 1)
            dve.memset(state[:], 0.0)
            dve.memset(tail[:], 0.0)
            dve.memset(row[:], 0.0)
            dve.memset(kn[:], 0.0)
            dve.memset(vt[:], 0.0)
            dve.wait_ge(par_loaded, 16)
            dve.tensor_scalar(nsink[:], prm[:, C_SINK:C_SINK + 8], -1.0, None, ALU.mult)
            dve.wait_ge(init_act, 1)
            dve.tensor_scalar(nalog[32:36], nalog[32:36], -1.0, None, ALU.mult).then_inc(init_done, 1)
            dve.wait_ge(init_done, 2)
            dve.sem_inc(w_lo.sem, SLOTS)
            dve.sem_inc(res.sem, 1)
            dve.sem_inc(fb_ready.sem, 2)
            dve.sem_inc(ff_ready.sem, 2)
            split_lo(0, 0)

            for k in range(KT):
                acc_add(N1, 0, k)
            dve.wait_ge(N1["rt_ready"].sem, N1["rt_ready"].after(0, 1))
            for k in range(KT + 1):
                if k < KT:
                    n1_norm(0, k)
                if k:
                    n1_low(0, k - 1)

            with dve.Fori(0, GROUPS) as g:
                with dve.Fori(0, CONV // 4) as i:
                    for s in range(4):
                        m = i * 4 + s
                        split_lo(g, i * 4, s + 1)
                        dve.wait_ge(raw_ready.sem, raw_ready.after(g, m * 3 + 3))
                        dve.wait_ge(silu_done.sem, silu_done.after(g, m - 1))
                        dve.tensor_scalar(cy[:, s % 2], raw[:, s % 2, 0:TOK], convw(prm, m, 0), None,
                                          ALU.mult).then_inc(tap_done.sem, 1)
                        for j in range(1, 4):
                            own(tap_done, g, m * 4 + j)
                            dve.scalar_tensor_tensor(out=cy[:, s % 2], in0=raw[:, s % 2, j:j + TOK],
                                                     scalar=convw(prm, m, j), in1=cy[:, s % 2],
                                                     op0=ALU.mult, op1=ALU.add).then_inc(tap_done.sem, 1)
                for m in range(GATE):
                    split_lo(g, CONV, m + 1)

                def src(n):
                    return qkvz[:, n, :] if n < 8 else akr[:] if n == 8 else aq[:, n - 9]

                def norm_square(n):
                    if n == 0:
                        dve.wait_ge(silu_done.sem, silu_done.after(g, 8))
                    if n >= 8:
                        dve.wait_ge(copied.sem, copied.after(g, n - 6))
                    dve.tensor_tensor(nq[:, n % 2], src(n), src(n), ALU.mult).then_inc(nsq_ready.sem, 1)

                def norm_apply(n):
                    dve.wait_ge(nrr_ready.sem, nrr_ready.after(g, n + 1))
                    dst = kn[:, HD:] if n == 8 else src(n)
                    scale = (float(P) ** -0.5 if n < 4 else 1.0 if n < 8 else
                             prm[:, C_KN:C_KN + 1] if n == 8 else prm[:, C_QN:C_QN + 1])
                    if n == 8:
                        dve.tensor_copy(kn[:, 0:HD], kn[:, TOK:]).then_inc(normed.sem, 1)
                        own(normed, g, 9)
                    dve.scalar_tensor_tensor(out=dst, in0=src(n), scalar=scale, in1=rr[:, n % 2],
                                             op0=ALU.mult, op1=ALU.mult).then_inc(normed.sem, 1)

                rd = [0]

                def row_step(ins):
                    ins.then_inc(row_dve.sem, 1)
                    rd[0] += 1
                    own(row_dve, g, rd[0])

                split_lo(g, U_BA, 1)
                norm_square(0)
                norm_square(1)
                dve.wait_ge(row_act.sem, row_act.after(g, 1))
                row_step(dve.scalar_tensor_tensor(out=rw[32:64, 1], in0=rw[32:64, 0], scalar=-1.0, in1=rw[32:64, 0],
                                                  op0=ALU.mult, op1=ALU.max))
                norm_apply(0)
                norm_square(2)
                split_lo(g, U_BA, 2)
                norm_apply(1)
                norm_square(3)
                dve.wait_ge(row_act.sem, row_act.after(g, 3))
                row_step(dve.tensor_scalar(U, E, 1.0, None, ALU.add))
                row_step(dve.scalar_tensor_tensor(out=E, in0=U, scalar=-1.0, in1=E, op0=ALU.add, op1=ALU.subtract))
                norm_apply(2)
                norm_square(4)
                split_lo(g, U_BA, 3)
                norm_apply(3)
                norm_square(5)
                norm_apply(4)
                norm_square(6)

                def rows_end():
                    dve.wait_ge(row_act.sem, row_act.after(g, 5))
                    row_step(dve.tensor_copy(row[0:4], rw[0:4, 2]))
                    row_step(dve.tensor_tensor(E, E, U, ALU.mult))
                    row_step(dve.tensor_tensor(L, L, E, ALU.subtract))
                    row_step(dve.scalar_tensor_tensor(out=L, in0=X, scalar=0.0, in1=L, op0=ALU.max, op1=ALU.add))
                    row_step(dve.tensor_scalar(rw[A4, 3], rw[A4, 3], nalog[A4], None, ALU.mult))
                    for t in range(TILES):
                        tile = slice(t * P, t * P + P)
                        row_step(dve.tensor_tensor_scan(row[A4, tile], cst[A4, K_ONE, :], rw[A4, 3, tile], 0.0,
                                                        ALU.mult, ALU.add))
                    assert rd[0] == row_dve.per_group

                for j in range(PAIRS):
                    split_lo(g, U_BA, 4 + j)
                    norm_apply(5 + 2 * j)
                    norm_square(7 + 2 * j) if 7 + 2 * j < NORMS else None
                    norm_apply(6 + 2 * j) if j < 3 else None
                    norm_square(8 + 2 * j) if 8 + 2 * j < NORMS else None
                    if j == 1:
                        rows_end()
                norm_apply(12)
                dve.memset(pp[:, :, :, 0:HD], 0.0).then_inc(pads.sem, 1)
                split_lo(g, U_BA, 8)

                def scores(n):
                    b, j = n % 2, n % PAIRS
                    dve.wait_ge(A["p_sc"].sem, A["p_sc"].after(g, n + 1))
                    var = (g + 3) // 4 if n < PAIRS else 1
                    if n == 0:
                        dve.wait_ge(bias_loaded, 16)
                    dve.scalar_tensor_tensor(out=ss[:, b], in0=ps[:, SC0:SC0 + 2, 0:KEYS], scalar=HD ** -0.5,
                                             in1=bia[:, var, j], op0=ALU.mult, op1=ALU.add).then_inc(A["ss_r"].sem, 1)
                    own(A["ss_r"], g, n + 1)
                    dve.tensor_reduce(att[:, b, MAX], ss[:, b], AX.X, ALU.max).then_inc(A["amax"].sem, 1)
                    own(A["amax"], g, n + 1)
                    sink = nsink[:, 2 * j:2 * j + 2]
                    dve.scalar_tensor_tensor(out=att[:, b, NMAX], in0=att[:, b, MAX], scalar=-1.0,
                                             in1=sink, op0=ALU.mult, op1=ALU.min).then_inc(A["nmax"].sem, 1)
                    own(A["nmax"], g, n + 1)
                    dve.tensor_tensor(att[:, b, SDIF], att[:, b, NMAX], sink, ALU.subtract).then_inc(A["sdiff"].sem, 1)

                def softmax(n):
                    b = n % 2
                    dve.wait_ge(A["es_r"].sem, A["es_r"].after(g, n + 1))
                    dve.tensor_tensor(att[:, b, RDEN], att[:, b, SUM], att[:, b, SEXP], ALU.add).then_inc(A["den_r"].sem, 1)
                    own(A["den_r"], g, n + 1)
                    dve.reciprocal(att[:, b, RDEN], att[:, b, RDEN]).then_inc(A["rden"].sem, 1)
                    own(A["rden"], g, n + 1)
                    dve.tensor_tensor(pp[:, b, :, HD:], pp[:, b, :, HD:],
                                      att[:, b, RDEN].unsqueeze(2).to_broadcast([P, 2, KEYS]),
                                      ALU.mult).then_inc(A["p_ready"].sem, 1)

                for q in range(TILES // 2):
                    def tick(k):
                        if k < 2 * PAIRS:
                            scores(q * 2 * PAIRS + k)
                        if 0 <= k - 1 < 2 * PAIRS:
                            softmax(q * 2 * PAIRS + k - 1)

                    def att_out(a):
                        t = 2 * q + a
                        tile = slice(t * P, t * P + P)
                        dve.wait_ge(ahi.sem, ahi.after(g, t + 1))
                        dve.tensor_tensor(h_l[:, 4:8, tile], heads(OV), h_h[:, 4:8, tile].bitcast(F32),
                                          ALU.subtract).then_inc(alo.sem, 1)

                    def w(s, a):
                        dve.wait_ge(s.sem, s.after(g, 2 * q + a + 1))

                    def w2(s):
                        dve.wait_ge(s.sem, s.after(g, q + 1))

                    if q == 0:
                        dve.wait_ge(B1["p_rowt"].sem, B1["p_rowt"].after(g, 1))
                        dve.tensor_copy(sm[:, :, 0:8].rearrange("p t (c h) -> p t c h", c=2),
                                        ps[:, PT, 0:256].rearrange("p (t c h) -> p t c h", t=TILES, c=2)[:, :, :, 0:4]
                                        ).then_inc(B1["tok"].sem, 1)
                        own(B1["tok"], g, 1)
                        dve.tensor_scalar(sm[:, :, NGC], sm[:, :, GC], -1.0, None, ALU.mult).then_inc(B1["ng"].sem, 1)
                    for a in range(2):
                        w(B["p_gr"], a)
                        dve.tensor_tensor(d1[:, a], heads(ring(a, 0)), per_head(cst[:, K_CAUS, :]),
                                          ALU.add).then_inc(B["dta_r"].sem, 1)
                        t = 2 * q + a
                        dve.tensor_tensor(sm[:, t, DGC].unsqueeze(2), heads(ring(a, 0))[:, :, P - 1:P],
                                          sm[:, t, GC].unsqueeze(2), ALU.subtract).then_inc(B["d2"].sem, 1)
                    tick(0)
                    if q == 0:
                        own(B1["egt"], g, 1)
                        dve.scalar_tensor_tensor(out=sm[:, :, CB], in0=sm[:, :, EGC], scalar=-1.0, in1=sm[:, :, BETA],
                                                 op0=ALU.mult, op1=ALU.mult).then_inc(B1["c1"].sem, 1)
                    for a in range(2):
                        w(B["p_br"], a)
                        w(B["dt_r"], a)
                        dve.tensor_tensor(d1[:, a], heads(ring(a, 1)), dt_[:, a], ALU.mult).then_inc(B["db_r"].sem, 1)
                        w(B["db_r"], a)
                        w(B["p_gg"], a)
                        dve.tensor_tensor(at_[:, a], heads(ring(a, 0)), d1[:, a], ALU.mult).then_inc(B["at_r"].sem, 1)
                        w(B["at_r"], a)
                        dve.tensor_tensor(xi[:, a], at_[:, a], per_head(cst[:, K_M0, :]), ALU.mult).then_inc(B["x0a"].sem, 1)
                        w(B["x0a"], a)
                        dve.tensor_tensor(xi[:, a], xi[:, a], per_head(I), ALU.add).then_inc(B["x0"].sem, 1)
                    for a in range(2):
                        w(B["p_kq"], a)
                        dve.tensor_tensor(qk[:, a], heads(ring(a, 1)), dt_[:, a], ALU.mult).then_inc(B["qk_r"].sem, 1)

                    def key_value(a):
                        t = 2 * q + a
                        tile = slice(t * P, t * P + P)
                        w(B["p_vt"], a)
                        dve.tensor_tensor(qkvz[:, 8:12, tile], heads(OV), wide(sm[:, t, BETA]), ALU.mult).then_inc(B["vb_r"].sem, 1)
                        w(B["p_kt"], a)
                        own(B1["c1"], g, 1)
                        dve.tensor_tensor(kb[:, a], heads(PT), wide(sm[:, t, CB]), ALU.mult).then_inc(B["kb_r"].sem, 1)
                        w2(B2["c2"])
                        dve.tensor_tensor(qkvz[:, 4:8, tile], heads(PT), wide(sm[:, t, CD]), ALU.mult).then_inc(B["kd_r"].sem, 1)

                    key_value(0)
                    tick(1)
                    key_value(1)
                    for l in range(LEVELS):
                        for a in range(2):
                            n = q * 2 * LEVELS + 2 * l + a
                            dve.wait_ge(p_y.sem, p_y.after(g, n + 1))
                            dve.tensor_tensor(flat(d1[:, a])[:, 0:256].rearrange("p (h c) -> p h c", h=HEADS),
                                              ps[:, ring(a, 3 * l + (l == 0)), 0:256].rearrange("p (h c) -> p h c", h=HEADS),
                                              cst_lev(cst, l).unsqueeze(1).to_broadcast([P, HEADS, 64]),
                                              ALU.mult).then_inc(y_ready.sem, 1)
                        if 2 + 2 * l <= 10:
                            tick(2 + 2 * l)
                        if l in (2, 4):
                            att_out(l // 4)
                        for a in range(2):
                            n = q * 2 * LEVELS + 2 * l + a
                            dve.wait_ge(p_u.sem, p_u.after(g, n + 1))
                            tc = first_half(flat(ti[:, a]), l)
                            dve.tensor_tensor(tc, ps[:, ring(a, 3 * l + 2), 0:256].rearrange("p (n b) -> p n b", b=2 << l),
                                              tc, ALU.add).then_inc(t_ready.sem, 1)
                        if 3 + 2 * l <= 9:
                            tick(3 + 2 * l)

                    def new_state(a):
                        w(B["p_su"], a)
                        for h in range(HEADS):
                            dve.scalar_tensor_tensor(out=state[:, h], in0=state[:, h], scalar=eg[:, a, h, P - 1:P],
                                                     in1=heads(ring(a, 1))[:, h], op0=ALU.mult,
                                                     op1=ALU.add).then_inc(s_ready.sem, 1)

                    def gated(a):
                        t = 2 * q + a
                        w(B["orr"], a)
                        dve.wait_ge(s_ready.sem, s_ready.after(g, (t + 1) * HEADS))
                        dve.scalar_tensor_tensor(out=eg[:, a], in0=heads(ring(a, 0)), scalar=prm[:, C_GN:C_GN + 1],
                                                 in1=dt_[:, a], op0=ALU.mult, op1=ALU.mult).then_inc(B["o1"].sem, 1)
                        w(B["o1"], a)
                        dve.tensor_tensor(eg[:, a], eg[:, a], qkvz[:, 12:16, t * P:t * P + P], ALU.mult).then_inc(B["o2"].sem, 1)

                    def mix_lo(a):
                        t = 2 * q + a
                        tile = slice(t * P, t * P + P)
                        w(B["mhi"], a)
                        dve.tensor_tensor(h_l[:, 0:4, tile], eg[:, a], h_h[:, 0:4, tile].bitcast(F32),
                                          ALU.subtract).then_inc(B["mlo"].sem, 1)

                    new_state(0)
                    gated(0)
                    new_state(1)
                    mix_lo(0)
                    gated(1)
                    mix_lo(1)

                dve.wait_ge(x_loaded.sem, x_loaded.after(g, 1))
                for m in range(KT):
                    split_lo(g, U_OUT, m + 1)
                    dve.wait_ge(unit_done.sem, unit_done.after(g, U_OUT + m + 1))
                    dve.tensor_tensor(xs[:, m], ps[:, m % 2, :], xs[:, m], ALU.add).then_inc(res.sem, 1)
                    if m:
                        acc_add(N2, g, m - 1)
                for k in range(KT):
                    dve.wait_ge(N2["hh_ready"].sem, N2["hh_ready"].after(g, k + 1))
                    dve.scalar_tensor_tensor(out=h_l[:, k], in0=xs[:, k], scalar=prm[:, C_N2 + k:C_N2 + k + 1],
                                             in1=h_h[:, k].bitcast(F32), op0=ALU.mult,
                                             op1=ALU.subtract).then_inc(N2["h_ready"].sem, 1)
                    if k == 2:
                        acc_add(N2, g, KT - 1)

                def up(half, i, s, first=False):
                    n = i * 4 + (half * 16 + s)
                    u = i * 4 + (U_MLP + 32 * half)
                    split_lo(g, u, s + 1)
                    if first:
                        dve.wait_ge(N2["rt_ready"].sem, N2["rt_ready"].after(g, 1))
                    dve.wait_ge(unit_done.sem, unit_done.after(g, u + (s + 1)))
                    dve.scalar_tensor_tensor(out=fb[:, s % 2], in0=ps[:, s % 2, :], scalar=0.0, in1=rt[:],
                                             op0=ALU.max, op1=ALU.mult).then_inc(fb_ready.sem, 1)
                    own(fb_ready, g, n + 1)
                    own(ff_ready, g, n - 1)
                    dve.tensor_tensor(ff[:, s % 2], fb[:, s % 2], fb[:, s % 2], ALU.mult).then_inc(fp_ready.sem, 1)
                    own(fp_ready, g, n + 1)
                    dve.wait_ge(fh_ready.sem, fh_ready.after(g, n + 1))
                    dve.tensor_tensor(ff_l[:, i * 4 + s, :], ff[:, s % 2], ff_h[:, i * 4 + s, :].bitcast(F32),
                                      ALU.subtract).then_inc(ff_ready.sem, 1)

                def down(half, i, s):
                    u = i * 4 + (U_MLP + 16 + 32 * half)
                    split_lo(g, u, s + 1)
                    if s % 2:
                        m = i * 2 + s // 2
                        dve.wait_ge(unit_done.sem, unit_done.after(g, u + (s + 1)))
                        dve.tensor_tensor(xs[:, m, :], ps[:, s // 2 % 2, :], xs[:, m, :], ALU.add).then_inc(res.sem, 1)

                for s in range(4):
                    up(0, 0, s, s == 0)
                with dve.Fori(1, 4) as i:
                    for s in range(4):
                        up(0, i, s)
                with dve.Fori(0, 4) as i:
                    for s in range(4):
                        down(0, i, s)
                with dve.Fori(0, 4) as i:
                    for s in range(4):
                        up(1, i, s)
                for s in range(16):
                    down(1, 0, s)
                    if 4 <= s < 8:
                        acc_add(N1, g + 1, 2 * s - 8)
                        acc_add(N1, g + 1, 2 * s - 7)
                    if s == 9:
                        dve.wait_ge(N1["rt_ready"].sem, N1["rt_ready"].after(g + 1, 1))
                    if 10 <= s < 14:
                        for k in (2 * s - 20, 2 * s - 19):
                            n1_norm(g + 1, k)
                        for k in (2 * s - 20, 2 * s - 19):
                            n1_low(g + 1, k)

        @block.tensor
        def _(pe):
            def mm(o, a, b, start=True, stop=True):
                return pe.matmul(o, a, b, start=start, stop=stop)

            def unit(g, u, n, bank, rhs, start=True, stop=True, first=None, order=range(KT)):
                b = n % 2
                r_h, r_l = rhs
                pe.wait_ge(w_lo.sem, w_lo.after(g, u + (n + 1)))
                o = ps[:, bank, :]
                for k in order:
                    if first:
                        first(k)
                    mm(o, w_h[:, b, k], r_h(k), start and k == order[0], False)
                    mm(o, w_h[:, b, k], r_l(k), False, False)
                    last = mm(o, w_l[:, b, k], r_h(k), False, stop and k == order[-1])
                last.then_inc(unit_done.sem, 1)

            hid = (lambda k: h_h[:, k], lambda k: h_l[:, k])

            pe.wait_ge(const_loaded, 16)
            pe.wait_ge(init_done, 2)
            pe.sem_inc(unit_done.sem, 2)

            def mean(N, g):
                pe.wait_ge(N["acc_ready"].sem, N["acc_ready"].after(g, KT))
                mm(ps[:, OV, :], cst[:, K_MEANX, :], acc[:]).then_inc(N["mean_done"].sem, 1)

            mean(N1, 0)
            with pe.Fori(0, GROUPS) as g:
                def n1_ready(k):
                    pe.wait_ge(N1["h_ready"].sem, N1["h_ready"].after(g, k + 1))

                with pe.Fori(0, CONV // 4) as i:
                    for s in range(4):
                        pe.wait_ge(raw_ready.sem, raw_ready.after(g, (i * 4 + s) * 3 - 3))
                        unit(g, i * 4, s, A0 + s % 2, hid, first=n1_ready if s == 0 else None)
                for m in range(GATE):
                    if m < 2:
                        pe.wait_ge(raw_ready.sem, raw_ready.after(g, (CONV + m) * 3 - 3))
                    else:
                        pe.wait_ge(z_ready.sem, z_ready.after(g, m - 1))
                    unit(g, CONV, m, A0 + m % 2, hid)

                def norm_sum(n):
                    pe.wait_ge(nsq_ready.sem, nsq_ready.after(g, n + 1))
                    mm(ps[:, NS + n % 2, :], cst[:, K_ONE if n < 8 else K_HALF, :], nq[:, n % 2]).then_inc(nsum_done.sem, 1)

                pe.wait_ge(z_ready.sem, z_ready.after(g, 3))
                unit(g, U_BA, 0, A0, hid)
                norm_sum(0)
                pe.wait_ge(z_ready.sem, z_ready.after(g, 4))
                unit(g, U_BA, 1, A0 + 1, hid)
                norm_sum(1)
                norm_sum(2)
                pe.wait_ge(row_act.sem, row_act.after(g, 2))
                unit(g, U_BA, 2, A0, hid)
                norm_sum(3)
                norm_sum(4)
                pe.wait_ge(copied.sem, copied.after(g, 1))
                for t in range(TILES):
                    last = pe.transpose(heads(OV)[:, t], avr[:, t * P:t * P + P], I)
                last.then_inc(vt_sum.sem, 1)
                for j in range(PAIRS):
                    pe.wait_ge(copied.sem, copied.after(g, j + 1))
                    unit(g, U_BA, 3 + j, A0 + (U_AQ + j) % 2, hid)
                    norm_sum(5 + 2 * j)
                    norm_sum(6 + 2 * j)

                def sc(n):
                    t, j = n // PAIRS, n % PAIRS
                    if n:
                        pe.wait_ge(A["ss_r"].sem, A["ss_r"].after(g, n))
                    for e in range(2):
                        r = slice(HD * e, HD * e + HD)
                        last = mm(ps[:, SC0 + e, 0:KEYS], aq[r, j, t * P:t * P + P], kn[r, t * P:t * P + KEYS])
                    last.then_inc(A["p_sc"].sem, 1)

                def pt(n):
                    pe.wait_ge(A["p_ready"].sem, A["p_ready"].after(g, n + 1))
                    o = ps[:, PT, :].rearrange("p (e c k) -> p e c k", e=2, c=2)
                    for e in range(2):
                        for c in range(2):
                            last = pe.transpose(o[:, e, c], pp[:, n % 2, e, c * P:c * P + P], I)
                    last.then_inc(A["p_pt"].sem, 1)

                def ov(n):
                    t, j = n // PAIRS, n % PAIRS
                    pe.wait_ge(A["ptc"].sem, A["ptc"].after(g, n + 1))
                    if n == 0:
                        pe.wait_ge(vt_ready.sem, vt_ready.after(g, 2))
                    if t and j == 0:
                        pe.wait_ge(alo.sem, alo.after(g, t))
                    for e in range(2):
                        r = slice(HD * e, HD * e + HD)
                        for c in range(2):
                            last = mm(heads(OV)[r, j], vt[:, t + c, r], pts[:, n % 2, e, c], c == 0, c == 1)
                    if j == PAIRS - 1:
                        last.then_inc(p_ov.sem, 1)

                pe.wait_ge(normed.sem, normed.after(g, NORMS + 1))
                pe.wait_ge(row_dve.sem, row_dve.after(g, row_dve.per_group))
                for q in range(TILES // 2):
                    def tick(k):
                        if k < 2 * PAIRS:
                            sc(q * 2 * PAIRS + k)
                        if 0 <= k - 3 < 2 * PAIRS:
                            ov(q * 2 * PAIRS + k - 3)
                        if 0 <= k - 2 < 2 * PAIRS:
                            pt(q * 2 * PAIRS + k - 2)

                    def w(s, a):
                        pe.wait_ge(s.sem, s.after(g, 2 * q + a + 1))

                    def four(o, f, sig):
                        for h in range(HEADS):
                            last = f(o[:, h], h)
                        last.then_inc(sig.sem, 1)

                    def part(i, a):
                        return qkvz[:, 4 * i:4 * i + 4, (2 * q + a) * P:(2 * q + a + 1) * P]

                    tick(0)
                    if q == 0:
                        for t in range(TILES):
                            last = pe.transpose(ps[:, PT, 64 * t:64 * t + 64], row[0:64, t * P:(t + 1) * P],
                                                cst[0:64, K_ID, 0:64])
                        last.then_inc(B1["p_rowt"].sem, 1)
                    for a in range(2):
                        if q:
                            w(B["o1"], a - 2)
                        four(heads(ring(a, 0)), lambda o, h: mm(o, cst[0:64, K_SEL + 4 + h, :], row[0:64, (2 * q + a) * P:(2 * q + a + 1) * P]), B["p_gr"])
                        four(heads(ring(a, 1)), lambda o, h: mm(o, cst[0:64, K_SEL + h, :], row[0:64, (2 * q + a) * P:(2 * q + a + 1) * P]), B["p_br"])

                    def transposes(a):
                        four(heads(PT), lambda o, h: pe.transpose(o, part(1, a)[:, h], I), B["p_kt"])
                        four(heads(OV), lambda o, h: pe.transpose(o, part(2, a)[:, h], I), B["p_vt"])

                    for a in range(2):
                        w(B["eg_r"], a)
                        four(heads(ring(a, 0)), lambda o, h: mm(o, part(1, a)[:, h], part(1, a)[:, h]), B["p_gg"])
                    if q == 0:
                        pe.wait_ge(B1["tok"].sem, B1["tok"].after(g, 1))
                    else:
                        w(B["oln"], -1)
                    transposes(0)
                    for a in range(2):
                        w(B["db_r"], a)
                        four(heads(ring(a, 1)), lambda o, h: mm(o, part(1, a)[:, h], part(0, a)[:, h]), B["p_kq"])
                    for a in range(2):
                        w(B["x0"], a)
                        four(heads(ring(a, 0)), lambda o, h: pe.transpose(o, xi[:, a, h], I), B["p_t0"])
                    tick(1)
                    w(B["kd_r"], 0)
                    transposes(1)
                    for l in range(LEVELS + 1):
                        n = q * 2 * LEVELS + 2 * l
                        for a in range(2 if l < LEVELS else 0):
                            if l == 0:
                                w(B["t0"], a)
                                w(B["qk_r"], a)
                            else:
                                pe.wait_ge(t_ready.sem, t_ready.after(g, n - 2 + a + 1))
                            o = ps[:, ring(a, 3 * l + (l == 0)), 0:256].rearrange("p (h n b) -> p h n b", h=HEADS, b=2 << l)
                            four(o, lambda o, h: mm(o, at_[:, a, h], first_half(ti[:, a, h], l)), p_y)
                        for a in range(2 if l else 0):
                            pe.wait_ge(t_ready.sem, t_ready.after(g, n - 2 + a + 1))
                            four(heads(ring(a, 3 * l + 1)), lambda o, h: pe.transpose(o, ti[:, a, h], I), p_x)
                        if l == 0:
                            w(B["kd_r"], 1)
                        if 2 + 2 * l <= 10:
                            tick(2 + 2 * l)
                        for a in range(2 if l < LEVELS else 0):
                            if l:
                                pe.wait_ge(x_ready.sem, x_ready.after(g, n - 2 + a + 1))
                            pe.wait_ge(y_ready.sem, y_ready.after(g, n + a + 1))
                            o = ps[:, ring(a, 3 * l + 2), 0:256].rearrange("p (h c) -> p h c", h=HEADS)
                            four(o, lambda o, h: mm(o, xi[:, a, h], flat(d1[:, a])[:, 64 * h:64 * h + 64]), p_u)
                        if 3 + 2 * l <= 9:
                            tick(3 + 2 * l)
                    for a in range(2):
                        pe.wait_ge(x_ready.sem, x_ready.after(g, (q + 1) * 2 * LEVELS - 1 + a))
                        four(heads(ring(a, 0)), lambda o, h: mm(o, kb[:, a, h], xi[:, a, h]), B["p_wt"])

                    def values(a):
                        w(B["wtc"], a)
                        if 2 * q + a:
                            pe.wait_ge(s_ready.sem, s_ready.after(g, (2 * q + a) * HEADS))
                        o = heads(ring(a, 1))
                        for h in range(HEADS):
                            mm(o[:, h], xi[:, a, h], part(2, a)[:, h], True, False)
                            last = mm(o[:, h], ti[:, a, h], state[:, h], False, True)
                        last.then_inc(B["p_vv"].sem, 1)

                    def state_and_out(a):
                        w(B["vnc"], a)
                        w(B["qd_r"], a)
                        o = heads(ring(a, 0))
                        for h in range(HEADS):
                            mm(o[:, h], state[:, h], part(0, a)[:, h], True, False)
                            last = mm(o[:, h], d1[:, a, h], qk[:, a, h], False, True)
                        last.then_inc(B["p_oo"].sem, 1)
                        four(heads(ring(a, 1)), lambda o, h: mm(o, part(1, a)[:, h], d1[:, a, h]), B["p_su"])

                    def out_mean(a):
                        w(B["osq_r"], a)
                        if a:
                            w(B["oln"], 0)
                        mm(ps[:, PT, :], cst[:, K_MEAN, :], flat(at_[:, a])).then_inc(B["p_on"].sem, 1)

                    values(0)
                    state_and_out(0)
                    values(1)
                    out_mean(0)
                    state_and_out(1)
                    out_mean(1)

                last = pe.transpose(ps[:, SC0, 0:P], I, I)
                last.then_inc(unit_done.sem, 1)
                def mix_ready(k):
                    if k == HEADS:
                        pe.wait_ge(alo.sem, alo.after(g, TILES))
                    if k == 0:
                        pe.wait_ge(B["mlo"].sem, B["mlo"].after(g, TILES))

                for m in range(KT):
                    if m >= 2:
                        pe.wait_ge(res.sem, res.after(g, m - 1))
                    unit(g, U_OUT, m, m % 2, hid, first=mix_ready if m == 0 else None,
                         order=(4, 5, 6, 7, 0, 1, 2, 3))

                def up(half, i, s):
                    pe.wait_ge(fb_ready.sem, fb_ready.after(g, i * 4 + (16 * half + s - 1)))
                    if half and s == 1:
                        pe.wait_ge(res.sem, res.after(g, 2 * KT))
                    unit(g, i * 4 + (U_MLP + 32 * half), s, s % 2, hid)

                def down(half, i, s):
                    kq = s % 2
                    if s == 2:
                        pe.wait_ge(fb_ready.sem, fb_ready.after(g, 16 * half + 16))
                    if kq == 0:
                        pe.wait_ge(res.sem, res.after(g, i * 2 + (KT + KT * half + s // 2 - 1)))
                    pe.wait_ge(ff_ready.sem, ff_ready.after(g, 16 * half + 8 * kq + 8))
                    hidden = (lambda k: ff_h[:, 8 * kq + k], lambda k: ff_l[:, 8 * kq + k])
                    unit(g, i * 4 + (U_MLP + 16 + 32 * half), s, s // 2 % 2, hidden, kq == 0, kq == 1)

                def next_ready(k):
                    pe.wait_ge(N2["h_ready"].sem, N2["h_ready"].after(g, k + 1))

                pe.wait_ge(res.sem, res.after(g, KT - 1))
                for s in range(4):
                    if s == 0:
                        unit(g, U_MLP, 0, 0, hid, first=next_ready)
                        mean(N2, g)
                    else:
                        if s == 1:
                            pe.wait_ge(res.sem, res.after(g, KT))
                        up(0, 0, s)
                with pe.Fori(1, 4) as i:
                    for s in range(4):
                        up(0, i, s)
                for half in range(2):
                    if half:
                        pe.wait_ge(res.sem, res.after(g, 2 * KT - 1))
                        pe.nop(nofuse=True)
                        with pe.Fori(0, 4) as i:
                            for s in range(4):
                                up(1, i, s)
                    pe.wait_ge(fb_ready.sem, fb_ready.after(g, 16 * half + 15))
                    pe.nop(nofuse=True)
                    for quarter in range(2):
                        with pe.Fori(2 * quarter, 2 * quarter + 2) as i:
                            for s in range(4):
                                down(half, i, s)
                        if half and quarter == 0:
                            mean(N1, g + 1)


def cst_lev(cst, l):
    return cst[:, K_LEV:K_LEV + 3, :].rearrange("p n c -> p (n c)")[:, 64 * l:64 * l + 64]


def convw(prm, m, j):
    return prm[:, C_CONV:C_CONV + 4 * CONV].rearrange("p (m j) -> p m j", j=4)[:, m, j:j + 1]


def u_div(u, n):
    return u // SLOTS + n // SLOTS



def constants():
    i = np.arange(P)
    c = np.zeros((P, N_CONST, P), np.float32)
    c[:, K_ID] = np.eye(P)
    c[:, K_ONE] = 1.0
    c[:, K_MEAN] = 1.0 / P
    c[:, K_MEANX] = 1.0 / D
    c[:, K_HALF] = (i[:, None] // HD == i[None, :] // HD) / HD
    c[:, K_CAUS] = np.where(i[:, None] <= i[None, :], 0.0, NEG)
    c[:, K_M0] = -1.0 * ((i[:, None] % 2 == 0) & (i[None, :] == i[:, None] + 1))
    for l in range(LEVELS):
        b = 2 << l
        j = i[i % (2 * b) < b]
        c[:, K_LEV + l // 2, 64 * (l % 2):64 * (l % 2) + 64] = -1.0 * (
            (i[:, None] // (2 * b) == j[None, :] // (2 * b)) & (i[:, None] % (2 * b) >= b))
    for h in range(HEADS):
        c[h, K_SEL + h] = 1.0
        c[32 + h, K_SEL + 4 + h] = 1.0
    q, k = i[:, None], np.arange(KEYS)[None, :]
    dist = np.abs(q + HD - k).astype(np.float32)
    seen = np.where(q < HD, k < 2 * HD, k >= HD)
    b = np.zeros((P, 2, PAIRS, 2, KEYS), np.float32)
    for j in range(PAIRS):
        for e in range(2):
            slope = np.float32(2.0 ** -(4 * e + j + 1))
            b[:, 0, j, e] = np.where(seen & (k >= HD), -slope * dist, NEG)
            b[:, 1, j, e] = np.where(seen, -slope * dist, NEG)
    return c.reshape(P, -1), b.reshape(P, -1)


def weight_units(w_in, w_out, w1, w2):
    def tile(m):
        return m.reshape(KT, P, P).transpose(1, 0, 2).reshape(P, KT * P)

    u = np.zeros((UNITS, P, KT * P), np.float32)
    for m in range(16):
        u[m] = tile(w_in[:, m * P:m * P + P])
    ba = np.zeros((D, P), np.float32)
    ba[:, 0:4] = w_in[:, 2048:2052]
    ba[:, 32:36] = w_in[:, 2052:2056]
    u[U_BA] = tile(ba)
    q0, k0, v0 = 2056, 2568, 2696
    for j in range(PAIRS):
        cols = [q0 + HD * h + c for h in (j, 4 + j) for c in range(HD)]
        u[U_AQ + j] = tile(w_in[:, cols])
    u[U_AK] = tile(w_in[:, k0:k0 + P])
    u[U_AV] = tile(w_in[:, v0:v0 + P])
    rows = list(range(512)) + [512 + HD * h + c for j in range(PAIRS) for h in (j, 4 + j) for c in range(HD)]
    wo = w_out[rows]
    for m in range(KT):
        cols = slice(m * P, m * P + P)
        u[U_OUT + m] = tile(wo[:, cols])
        for half in range(2):
            for kq in range(2):
                r = half * 2048 + kq * 1024
                u[U_MLP + 16 + 32 * half + 2 * m + kq] = tile(w2[r:r + 1024, cols])
    for m in range(32):
        u[U_MLP + 32 * (m // 16) + m % 16] = tile(w1[:, m * P:m * P + P])
    return u


def parameters(norm1_w, norm2_w, conv_w, gdn_norm_w, q_norm_w, k_norm_w, a_log, dt_bias, sinks):
    p = np.zeros((P, N_PAR), np.float32)
    p[:, C_N1:C_N1 + 8] = norm1_w[0].reshape(8, P).T
    p[:, C_N2:C_N2 + 8] = norm2_w[0].reshape(8, P).T
    p[:, C_CONV:C_CONV + 48] = conv_w[0].reshape(4, CONV, P).transpose(2, 1, 0).reshape(P, 48)
    p[:, C_GN] = gdn_norm_w[0]
    p[:, C_QN] = np.concatenate([q_norm_w[0]] * 2)
    p[:, C_KN] = np.concatenate([k_norm_w[0]] * 2)
    p[32:36, C_ALOG] = a_log[0]
    p[32:36, C_DT] = dt_bias[0]
    p[:, C_SINK:] = sinks[0].reshape(2, PAIRS).T.reshape(-1)[None, :]
    return p


def kernel(x, norm1_w, w_in, conv_w, a_log, dt_bias, gdn_norm_w, q_norm_w, k_norm_w, sinks, w_out, norm2_w, w1, w2):
    import concourse.bacc as bacc
    from concourse.bass_utils import run_bass_kernel_spmd

    (x, norm1_w, w_in, conv_w, a_log, dt_bias, gdn_norm_w, q_norm_w, k_norm_w, sinks, w_out, norm2_w, w1, w2) = (
        np.asarray(a) for a in (x, norm1_w, w_in, conv_w, a_log, dt_bias, gdn_norm_w, q_norm_w, k_norm_w, sinks,
                                w_out, norm2_w, w1, w2))
    con, bias = constants()
    arrays = {
        "x": np.ascontiguousarray(x[0].reshape(GROUPS, TOK, KT, P).transpose(0, 3, 2, 1)),
        "w": weight_units(w_in[0], w_out[0], w1[0], w2[0]),
        "par": parameters(norm1_w, norm2_w, conv_w, gdn_norm_w, q_norm_w, k_norm_w, a_log, dt_bias, sinks),
        "con": con.reshape(P, N_CONST, P),
        "bias": bias,
    }
    nc = bacc.Bacc("TRN2", target_bir_lowering=False, num_devices=1)
    ins = [nc.dram_tensor(n, a.shape, F32, kind="ExternalInput").ap() for n, a in arrays.items()]
    out = nc.dram_tensor("out", (GROUPS, P, KT, TOK), F32, kind="ExternalOutput").ap()
    build(nc, *ins, out)
    y = run_bass_kernel_spmd(nc, [arrays], core_ids=[0]).results[0]["out"]
    return np.ascontiguousarray(y.transpose(0, 3, 2, 1)).reshape(1, SEQ, D)
```

```python
import math

from contextlib import ExitStack

import numpy as np

import concourse.bass as bass
from concourse import mybir

F32 = mybir.dt.float32
F32R = mybir.dt.float32r
ALU = mybir.AluOpType
ACT = mybir.ActivationFunctionType
AX = mybir.AxisListType

P = 128
D = 1024
SEQ = 2048
TOK = 512
GROUPS = SEQ // TOK
TILES = TOK // P
KT = D // P
HEADS = 4
PAIRS = 4
HD = 64
KEYS = 192
LEVELS = 6
EPS = 1e-6
NEG = -1e30

CONV, GATE = 12, 4
U_BA, U_AV, U_AK, U_AQ = 16, 17, 18, 19
U_PAD, U_OUT, U_MLP = 23, 24, 32
UNITS = 96
NORMS = 13
SLOTS = 4
XPARTS = 4

C_N1, C_N2, C_CONV, C_GN, C_QN, C_KN, C_ALOG, C_DT, C_SINK = 0, 8, 16, 64, 65, 66, 67, 68, 69
N_PAR = C_SINK + 2 * PAIRS
K_ID, K_ONE, K_MEAN, K_MEANX, K_HALF, K_CAUS, K_M0, K_LEV, K_SEL = 0, 1, 2, 3, 4, 5, 6, 7, 10
N_CONST = K_SEL + 2 * HEADS


STEPS = (
    {"gram": (0,), "query": (1,), "level0": (2,), "level1": (3,), "level2": (4,), "level3": (5,),
     "level4": (6,), "level5": (7,), "w": (8,), "value": (9,)},
    {"before": (10,), "gram": (11,), "query": (12,), "level1": (13,), "level2": (14,), "level3": (15,),
     "level4": (16,), "level5": (17,), "w": (18,)},
)


def ends_tile(k):
    return k // PAIRS - 1 if k >= PAIRS and k % PAIRS == 2 else None


class Signal:

    def __init__(self, sem, per_group, credit=0, step=1):
        self.sem, self.per_group, self.credit, self.step = sem, per_group, credit, step

    def after(self, g, n):
        return g * (self.per_group * self.step) + n * self.step + self.credit


def build(nc, x, w, par, con, bias, out):
    with ExitStack() as ctx:
        def sb(name, shape, dt=F32, scope=ctx):
            return scope.enter_context(nc.sbuf_tensor(name, shape, dt))

        def signal(name, per_group, credit=0, step=1):
            return Signal(ctx.enter_context(nc.semaphore(name)), per_group, credit, step)

        stage = sb("stage", [P, SLOTS, KT, P])
        w_h = sb("w_h", [P, 2, KT, P], F32R)
        w_l = sb("w_l", [P, 2, KT, P], F32R)
        xs = sb("xs", [P, KT, TOK])
        h_h = sb("h_h", [P, KT, TOK], F32R)
        with ExitStack() as s:
            x_next = sb("x_next", [P, KT, TOK], F32, s)
        h_l = sb("h_l", [P, KT, TOK], F32R)
        aq = sb("aq", [P, PAIRS, TOK])
        kn = sb("kn", [P, HD + TOK])
        vt = sb("vt", [P, 1 + TILES, P])
        state = sb("state", [P, 2, HEADS, P])
        tail = sb("tail", [P, CONV, 3])
        row = sb("row", [64, TOK])
        cst = sb("cst", [P, N_CONST, P])
        bia = sb("bia", [P, 2, PAIRS, 2, KEYS])
        prm = sb("prm", [P, N_PAR])
        nalog = sb("nalog", [P, 1])
        nsink = sb("nsink", [P, 2 * PAIRS])
        eps = sb("eps", [P, 1])
        att = sb("att", [P, 2, 10])
        sm = sb("sm", [P, TILES, 28])
        with ExitStack() as s:
            ff_h = sb("ff_h", [P, 16, TOK], F32R, s)
            ff_l = sb("ff_l", [P, 16, TOK], F32R, s)
        qkvz = sb("qkvz", [P, 16, TOK])
        with ExitStack() as s:
            raw = sb("raw", [P, 2, 3 + TOK], F32, s)
            cy = sb("cy", [P, 2, TOK], F32, s)
            akr = sb("akr", [P, TOK], F32, s)
            avr = sb("avr", [P, TOK], F32, s)
            nq = sb("nq", [P, 2, TOK], F32, s)
            rr = sb("rr", [P, 2, TOK], F32, s)
            rw = sb("rw", [P, 4, TOK], F32, s)
        eg = sb("eg", [P, 2, HEADS, P])
        d1 = sb("d1", [P, 2, HEADS, P])
        dt_ = sb("dt", [P, 2, HEADS, P])
        at_ = sb("at", [P, 2, HEADS, P])
        xi = sb("xi", [P, 2, HEADS, P])
        ti = sb("ti", [P, 2, HEADS, P])
        kb = sb("kb", [P, 2, HEADS, P])
        qk = sb("qk", [P, 2, HEADS, P])
        with ExitStack() as s:
            sq = sb("sq", [P, 2, TOK], F32, s)
            acc = sb("acc", [P, TOK], F32, s)
            rt = sb("rt", [P, TOK], F32, s)
            ht = sb("ht", [P, 2, TOK], F32, s)
            fb = sb("fb", [P, 2, TOK], F32, s)
            ff = sb("ff", [P, 2, TOK], F32, s)
        ss = sb("ss", [P, 2, 2, KEYS])
        pp = sb("pp", [P, 2, 2, 256])
        pts = sb("pts", [P, 2, 2, 2, P])

        ps = ctx.enter_context(nc.psum_tensor("ps", [P, 8, 512], F32))
        SC, PT, OV, NS, A0 = 0, 2, 3, 1, 6

        def ring(a, k):
            return 4 + 2 * a + k % 2

        def heads(b):
            return ps[:, b, :].rearrange("p (h c) -> p h c", h=HEADS)

        I = cst[:, K_ID, :]
        R64, A4 = slice(0, 64), slice(32, 36)
        X, E, U, L = (rw[R64, i] for i in range(4))

        def wide(v):
            return v.unsqueeze(2).to_broadcast([P, HEADS, P])

        BETA, GC, NGC, DGC, EGC, CB, CD = (slice(4 * i, 4 * i + 4) for i in range(7))
        MAX, NMAX, SUM, SEXP, RDEN = (slice(2 * i, 2 * i + 2) for i in range(5))

        def rows_bank():
            return ps[:, SC:SC + 2, 2 * P:].rearrange("p b (h c) -> p b h c", h=2)

        def two_by_two(m):
            return m.rearrange("p (b h) c -> p b h c", b=2)

        def first_half(m, l):
            return m.rearrange("p (n two b) -> p n two b", two=2, b=2 << l)[:, :, 0, :]

        def flat(m):
            return m.rearrange("p h c -> p (h c)")

        def per_head(m):
            return m.unsqueeze(1).to_broadcast([P, HEADS, P])

        par_loaded = ctx.enter_context(nc.semaphore("par_loaded"))
        const_loaded = ctx.enter_context(nc.semaphore("const_loaded"))
        bias_loaded = ctx.enter_context(nc.semaphore("bias_loaded"))
        init_done = ctx.enter_context(nc.semaphore("init_done"))
        init_act = ctx.enter_context(nc.semaphore("init_act"))
        w_loaded = [signal(f"w_loaded{i}", UNITS // SLOTS, step=16) for i in range(SLOTS)]
        w_hi = signal("w_hi", UNITS)
        w_lo = signal("w_lo", UNITS, credit=SLOTS)
        unit_done = signal("unit_done", UNITS, credit=2)
        x_loaded = signal("x_loaded", 1, step=16)
        next_loaded = [signal(f"next_loaded{i}", 1, step=16) for i in range(XPARTS)]
        y_stored = signal("y_stored", KT, step=16)
        N1, N2 = ({n: signal(f"{n}{i}", c) for n, c in
                   (("sq_ready", KT), ("acc_ready", KT), ("mean_done", 1), ("rt_ln", 1), ("rt_ready", 1),
                    ("hh_ready", KT), ("h_ready", KT))} for i in (1, 2))
        ht_ready = signal("ht_ready", KT)
        raw_ready = signal("raw_ready", 3 * CONV, credit=6)
        tap_done = signal("tap_done", 4 * CONV)
        silu_done = signal("silu_done", CONV, credit=2)
        z_ready = signal("z_ready", GATE)
        copied = signal("copied", 6)
        nsq_ready = signal("nsq_ready", NORMS)
        nsum_done = signal("nsum_done", NORMS)
        nln_done = signal("nln_done", NORMS)
        nrr_ready = signal("nrr_ready", NORMS)
        normed = signal("normed", NORMS + 1)
        row_act = signal("row_act", 5)
        row_dve = signal("row_dve", 8 + TILES)
        vt_sum = signal("vt_sum", 1)
        vt_ready = signal("vt_ready", 2)
        B = {n: signal(n, TILES) for n in
             ("p_gr p_br p_gg p_kt p_vt p_kq p_t0 p_wt p_vv p_oo p_su p_on "
              "dta_r d2 db_r at_r x0a x0 qk_r vb_r kb_r kd_r o1 o2 mlo "
              "eg_r dt_r t0 wtc vnc osq_r oln orr mhi qd_r").split()}
        B2 = {n: signal(n, 2) for n in ("c2",)}
        B1 = {n: signal(n, 1) for n in "p_rowt tok ng c1 egt".split()}
        p_y = signal("p_y", TILES * LEVELS)
        p_u = signal("p_u", TILES * LEVELS)
        p_x = signal("p_x", TILES * LEVELS)
        y_ready = signal("y_ready", TILES * LEVELS)
        t_ready = signal("t_ready", TILES * LEVELS)
        x_ready = signal("x_ready", TILES * LEVELS)
        s_ready = signal("s_ready", TILES * HEADS)
        A = {n: signal(n, TILES * PAIRS) for n in
             "p_sc p_pt ss_r amax nmax den_r rden p_ready es_r ptc".split()}
        p_ov = signal("p_ov", TILES)
        ahi = signal("ahi", TILES)
        alo = signal("alo", TILES)
        pads = signal("pads", 1)
        res = signal("res", KT + 2 * KT, credit=1)
        fb_ready = signal("fb_ready", 32, credit=2)
        fh_ready = signal("fh_ready", 32)
        fp_ready = signal("fp_ready", 32)
        ff_ready = signal("ff_ready", 32, credit=2)

        block = ctx.enter_context(nc.Block())

        @block.sync
        def _(sp):
            def load(u, s, dst_wait=None):
                sp.dma_start(stage[:, s], w[u].rearrange("p (k m) -> p k m", k=KT)).then_inc(w_loaded[s].sem, 16)

            sp.dma_start(prm[:], par).then_inc(par_loaded, 16)
            sp.dma_start(cst[:], con).then_inc(const_loaded, 16)
            with sp.Fori(0, GROUPS) as g:
                with sp.Fori(0, UNITS // SLOTS) as i:
                    for s in range(SLOTS):
                        sp.wait_ge(w_lo.sem, w_lo.after(g, i * SLOTS + (s + 1 - SLOTS)))
                        load(i * SLOTS + s, s)
            sp.wait_ge(w_lo.sem, w_lo.after(GROUPS, 1 - SLOTS))
            load(0, 0)

        @block.gpsimd
        def _(pool):
            def load_next(g):
                for i in range(XPARTS):
                    part = slice(i * (KT // XPARTS), (i + 1) * (KT // XPARTS))
                    pool.dma_start(x_next[:, part], x[g, :, part]).then_inc(next_loaded[i].sem, 16)

            load_next(0)
            pool.wait_ge(unit_done.sem, unit_done.after(0, 1))
            pool.dma_start(bia[:], bias.rearrange("p (v j e k) -> p v j e k", v=2, j=PAIRS, e=2)).then_inc(bias_loaded, 16)
            with pool.Fori(0, GROUPS) as g:
                pool.wait_ge(unit_done.sem, unit_done.after(g, 1))
                pool.nop(nofuse=True)
                pool.dma_start(xs[:], x[g]).then_inc(x_loaded.sem, 16)
                for q in range(TILES // 2):
                    def attend(stage):
                        for k in STEPS[q].get(stage, ()):
                            n = k - 1
                            if 0 <= n < TILES * PAIRS:
                                pool.wait_ge(A["rden"].sem, A["rden"].after(g, n + 1))
                                nc.gpsimd.tensor_tensor(pp[:, n % 2, :, HD:], pp[:, n % 2, :, HD:],
                                                        att[:, n % 2, RDEN].unsqueeze(2).to_broadcast([P, 2, KEYS]),
                                                        ALU.mult).then_inc(A["p_ready"].sem, 1)

                    def w(s, a):
                        pool.wait_ge(s.sem, s.after(g, 2 * q + a + 1))

                    attend("before")
                    for a in range(2):
                        w(B["x0a"], a)
                        nc.gpsimd.tensor_tensor(xi[:, a], xi[:, a], per_head(I), ALU.add).then_inc(B["x0"].sem, 1)
                    attend("gram")
                    attend("query")
                    for a in range(2):
                        q_tile = qkvz[:, 0:4, (2 * q + a) * P:(2 * q + a + 1) * P]
                        w(B["p_kq"], a)
                        nc.gpsimd.tensor_tensor(q_tile, q_tile, eg[:, a], ALU.mult).then_inc(B["qd_r"].sem, 1)
                    for l in range(LEVELS):
                        attend(f"level{l}")
                    attend("w")
                    attend("value")
                pool.wait_ge(unit_done.sem, unit_done.after(g, U_MLP + 32 + 16))
                pool.nop(nofuse=True)
                load_next((g + 1) % GROUPS)
                for m in range(KT):
                    pool.wait_ge(res.sem, res.after(g, 2 * KT + m + 1))
                    pool.nop(nofuse=True)
                    pool.dma_start(out[g, :, m], xs[:, m]).then_inc(y_stored.sem, 16)
                pool.wait_ge(y_stored.sem, y_stored.after(g, KT))
                pool.nop(nofuse=True)
            pool.wait_ge(x_loaded.sem, x_loaded.after(GROUPS, 0))
            for part in next_loaded:
                pool.wait_ge(part.sem, part.after(GROUPS, 1))

        @block.scalar
        def _(act):
            def split_hi(g, u, n=0):
                s, b = n % SLOTS, n % 2
                act.wait_ge(w_loaded[s].sem, w_loaded[s].after(g, u_div(u, n) + 1))
                act.wait_ge(unit_done.sem, unit_done.after(g, u + (n - 1)))
                act.copy(w_h[:, b], stage[:, s]).then_inc(w_hi.sem, 1)

            def square(N, g, k, src):
                if k >= 2:
                    act.wait_ge(N["acc_ready"].sem, N["acc_ready"].after(g, k - 1))
                act.activation(sq[:, k % 2], src, ACT.Square).then_inc(N["sq_ready"].sem, 1)

            def root(N, g):
                act.wait_ge(N["mean_done"].sem, N["mean_done"].after(g, 1))
                act.activation(rt[:], ps[:, OV, :], ACT.Ln, bias=eps[:, 0:1]).then_inc(N["rt_ln"].sem, 1)
                act.wait_ge(N["rt_ln"].sem, N["rt_ln"].after(g, 1))
                act.activation(rt[:], rt[:], ACT.Exp, scale=-0.5).then_inc(N["rt_ready"].sem, 1)

            def n1_square(g, k):
                part = next_loaded[k // (KT // XPARTS)]
                act.wait_ge(part.sem, part.after(g, 1))
                square(N1, g, k, x_next[:, k])

            def n1_high(g, k):
                act.wait_ge(ht_ready.sem, ht_ready.after(g, k + 1))
                act.copy(h_h[:, k], ht[:, k % 2]).then_inc(N1["hh_ready"].sem, 1)

            act.wait_ge(par_loaded, 16)
            act.wait_ge(init_done, 1)
            act.preload_act_table_set("natural_log_exp_and_others")
            act.activation(nalog[32:36], prm[32:36, C_ALOG:C_ALOG + 1], ACT.Exp).then_inc(init_act, 1)
            act.sem_inc(raw_ready.sem, 6)
            act.sem_inc(silu_done.sem, 2)
            split_hi(0, 0)
            for k in range(KT):
                n1_square(0, k)
            root(N1, 0)
            for k in range(KT):
                n1_high(0, k)

            with act.Fori(0, GROUPS) as g:
                act.preload_act_table_set("silu_and_others")

                def silu(m, s):
                    act.wait_ge(tap_done.sem, tap_done.after(g, m * 4 + 4))
                    act.activation(qkvz[:, m, :], cy[:, s % 2], ACT.Silu).then_inc(silu_done.sem, 1)

                def conv_input(i, s):
                    split_hi(g, i * 4, s + 1)
                    act.wait_ge(unit_done.sem, unit_done.after(g, i * 4 + s + 1))
                    act.copy(raw[:, s % 2, 3:], ps[:, A0 + s % 2, :]).then_inc(raw_ready.sem, 1)
                    act.copy(raw[:, s % 2, 0:3], tail[:, i * 4 + s, :]).then_inc(raw_ready.sem, 1)
                    act.wait_ge(raw_ready.sem, raw_ready.after(g, (i * 4 + s) * 3 + 2))
                    act.nop(nofuse=True)
                    act.copy(tail[:, i * 4 + s, :], ps[:, A0 + s % 2, TOK - 3:]).then_inc(raw_ready.sem, 1)

                for s in range(4):
                    conv_input(0, s)
                    if s:
                        silu(s - 1, s - 1)
                with act.Fori(1, CONV // 4) as i:
                    for s in range(4):
                        conv_input(i, s)
                        silu(i * 4 + (s - 1), s - 1)
                for m in range(GATE):
                    split_hi(g, CONV, m + 1)
                    if m == 0:
                        silu(CONV - 1, CONV - 1)
                    act.wait_ge(unit_done.sem, unit_done.after(g, CONV + m + 1))
                    act.activation(qkvz[:, 12 + m, :], ps[:, A0 + m % 2, :], ACT.Silu).then_inc(z_ready.sem, 1)

                act.preload_act_table_set("natural_log_exp_and_others")

                def norm_root(n):
                    act.wait_ge(nsum_done.sem, nsum_done.after(g, n + 1))
                    act.activation(rr[:, n % 2], ps[:, NS + (n + 1) % 2, :], ACT.Ln, bias=eps[:, 0:1]).then_inc(nln_done.sem, 1)
                    act.wait_ge(nln_done.sem, nln_done.after(g, n + 1))
                    act.activation(rr[:, n % 2], rr[:, n % 2], ACT.Exp, scale=-0.5).then_inc(nrr_ready.sem, 1)

                def wt(s, t):
                    act.wait_ge(s.sem, s.after(g, t + 1))

                def decay(t):
                    a = t % 2
                    wt(B["d2"], t)
                    act.activation(eg[:, a], heads(ring(a, 0)), ACT.Exp).then_inc(B["eg_r"].sem, 1)
                    for h in range(HEADS):
                        e = act.activation(dt_[:, a, h], d1[:, a, h], ACT.Exp, bias=sm[:, t, NGC][:, h:h + 1])
                    e.then_inc(B["dt_r"].sem, 1)

                split_hi(g, U_BA, 1)
                act.wait_ge(unit_done.sem, unit_done.after(g, U_BA + 1))
                act.activation(X, ps[R64, A0, :], ACT.Identity, bias=prm[R64, C_DT:C_DT + 1]).then_inc(row_act.sem, 1)
                act.copy(rw[0:32, 1], ps[0:32, A0, :]).then_inc(row_act.sem, 1)
                norm_root(0)
                split_hi(g, U_BA, 2)
                act.wait_ge(unit_done.sem, unit_done.after(g, U_AV + 1))
                act.copy(avr[:], ps[:, A0 + 1, :]).then_inc(copied.sem, 1)
                act.wait_ge(row_dve.sem, row_dve.after(g, 1))
                act.wait_ge(row_act.sem, row_act.after(g, 2))
                act.activation(E, E, ACT.Exp, scale=-1.0).then_inc(row_act.sem, 1)
                norm_root(1)
                norm_root(2)
                split_hi(g, U_BA, 3)
                act.wait_ge(unit_done.sem, unit_done.after(g, U_AK + 1))
                act.copy(akr[:], ps[:, A0, :]).then_inc(copied.sem, 1)
                act.wait_ge(row_dve.sem, row_dve.after(g, 2))
                act.activation(L, U, ACT.Ln).then_inc(row_act.sem, 1)
                norm_root(3)
                norm_root(4)
                act.copy(vt[:, 0], vt[:, TILES]).then_inc(vt_ready.sem, 1)
                act.wait_ge(vt_ready.sem, vt_ready.after(g, 1))
                act.wait_ge(vt_sum.sem, vt_sum.after(g, 1))
                act.copy(vt[:, 1:], heads(OV)).then_inc(vt_ready.sem, 1)
                for j in range(PAIRS):
                    split_hi(g, U_BA, 4 + j)
                    act.wait_ge(unit_done.sem, unit_done.after(g, U_AQ + j + 1))
                    act.copy(aq[:, j], ps[:, A0 + (U_AQ + j) % 2, :]).then_inc(copied.sem, 1)
                    if j == 0:
                        act.wait_ge(row_dve.sem, row_dve.after(g, 3))
                        act.wait_ge(row_act.sem, row_act.after(g, 4))
                        act.activation(U, L, ACT.Exp, scale=-1.0).then_inc(row_act.sem, 1)
                    norm_root(5 + 2 * j)
                    if j == PAIRS - 1:
                        act.wait_ge(B1["tok"].sem, B1["tok"].after(g, 1))
                        act.activation(sm[:, :, EGC], sm[:, :, GC], ACT.Exp).then_inc(B1["egt"].sem, 1)
                        act.wait_ge(B1["ng"].sem, B1["ng"].after(g, 1))
                        decay(0)
                        decay(1)
                    norm_root(6 + 2 * j)

                def exps(n):
                    b = n % 2
                    act.wait_ge(A["nmax"].sem, A["nmax"].after(g, n + 1))
                    if n == 0:
                        act.wait_ge(pads.sem, pads.after(g, 1))
                    for e in range(2):
                        act.activation(pp[:, b, e, HD:], ss[:, b, e], ACT.Exp, bias=att[:, b, NMAX][:, e:e + 1],
                                       accum_out=att[:, b, SUM][:, e:e + 1])
                    for e in range(2):
                        sink = C_SINK + 2 * (n % PAIRS) + e
                        last = act.activation(att[:, b, SEXP][:, e:e + 1], att[:, b, NMAX][:, e:e + 1], ACT.Exp,
                                              bias=prm[:, sink:sink + 1])
                    last.then_inc(A["es_r"].sem, 1)

                def pt_copy(n):
                    act.wait_ge(A["p_pt"].sem, A["p_pt"].after(g, n + 1))
                    act.copy(pts[:, n % 2], ps[:, PT, :].rearrange("p (e c k) -> p e c k", e=2, c=2)).then_inc(A["ptc"].sem, 1)

                def att_out(t):
                    act.wait_ge(p_ov.sem, p_ov.after(g, t + 1))
                    act.copy(h_h[:, 4:8, t * P:t * P + P], heads(OV)).then_inc(ahi.sem, 1)

                for q in range(TILES // 2):
                    def attend(stage):
                        for k in STEPS[q].get(stage, ()):
                            if ends_tile(k) is not None and stage != "before":
                                att_out(ends_tile(k))
                            if 0 <= k - 2 < TILES * PAIRS:
                                pt_copy(k - 2)
                            if k < TILES * PAIRS:
                                exps(k)

                    def w(s, a):
                        wt(s, 2 * q + a)

                    if q:
                        att_out(ends_tile(STEPS[q]["before"][0]))
                        for a in range(2):
                            decay(2 * q + a)
                    attend("before")
                    pair = slice(2 * q, 2 * q + 2)
                    act.activation(sm[:, pair, CD], sm[:, pair, DGC], ACT.Exp).then_inc(B2["c2"].sem, 1)
                    attend("gram")
                    for a in range(2):
                        w(B["p_t0"], a)
                        act.copy(ti[:, a], heads(ring(a, 0))).then_inc(B["t0"].sem, 1)
                    attend("query")
                    if q == 0:
                        split_hi(g, U_BA, 8)
                    for l in range(1, LEVELS + 1):
                        for a in range(2):
                            n = q * 2 * LEVELS + 2 * (l - 1) + a
                            act.wait_ge(p_x.sem, p_x.after(g, n + 1))
                            act.copy(xi[:, a], heads(ring(a, 3 * l + 1))).then_inc(x_ready.sem, 1)
                        attend(f"level{l - 1}")
                    for a in range(2):
                        w(B["p_wt"], a)
                        act.copy(ti[:, a], heads(ring(a, 0))).then_inc(B["wtc"].sem, 1)
                    attend("w")

                    def v_new(a):
                        w(B["p_vv"], a)
                        act.copy(d1[:, a], heads(ring(a, 1))).then_inc(B["vnc"].sem, 1)

                    def out_square(a):
                        w(B["p_oo"], a)
                        act.activation(at_[:, a], heads(ring(a, 0)), ACT.Square).then_inc(B["osq_r"].sem, 1)

                    def out_root(a):
                        w(B["p_on"], a)
                        act.activation(dt_[:, a], heads(PT), ACT.Ln, bias=eps[:, 0:1]).then_inc(B["oln"].sem, 1)
                        w(B["oln"], a)
                        act.activation(dt_[:, a], dt_[:, a], ACT.Exp, scale=-0.5).then_inc(B["orr"].sem, 1)

                    def mix_hi(a):
                        t = 2 * q + a
                        w(B["o2"], a)
                        act.copy(h_h[:, 0:4, t * P:t * P + P], eg[:, a]).then_inc(B["mhi"].sem, 1)

                    v_new(0)
                    attend("value")
                    out_square(0)
                    v_new(1)
                    out_root(0)
                    out_square(1)
                    mix_hi(0)
                    out_root(1)
                    mix_hi(1)

                for m in range(KT):
                    split_hi(g, U_OUT, m + 1)
                    if 0 < m < KT:
                        act.wait_ge(res.sem, res.after(g, m))
                        square(N2, g, m - 1, xs[:, m - 1])
                act.wait_ge(unit_done.sem, unit_done.after(g, U_OUT + KT))
                for k in range(KT):
                    act.activation(h_h[:, k], xs[:, k], ACT.Copy, scale=prm[:, C_N2 + k:C_N2 + k + 1]).then_inc(N2["hh_ready"].sem, 1)
                    if k == 1:
                        act.wait_ge(res.sem, res.after(g, KT))
                        square(N2, g, KT - 1, xs[:, KT - 1])

                def up(half, i, s, first=False):
                    n = i * 4 + (half * 16 + s)
                    split_hi(g, i * 4 + (U_MLP + 32 * half), s + 1)
                    if first:
                        root(N2, g)
                    act.wait_ge(fb_ready.sem, fb_ready.after(g, n + 1))
                    act.activation(ff_h[:, i * 4 + s, :], fb[:, s % 2], ACT.Square).then_inc(fh_ready.sem, 1)

                for s in range(4):
                    up(0, 0, s, s == 0)
                with act.Fori(1, 4) as i:
                    for s in range(4):
                        up(0, i, s)
                with act.Fori(0, 4) as i:
                    for s in range(4):
                        split_hi(g, i * 4 + (U_MLP + 16), s + 1)
                with act.Fori(0, 4) as i:
                    for s in range(4):
                        up(1, i, s)
                for s in range(16):
                    split_hi(g, U_MLP + 48, s + 1)
                    if 4 <= s < 8:
                        n1_square(g + 1, 2 * s - 8)
                        n1_square(g + 1, 2 * s - 7)
                    if s == 8:
                        root(N1, g + 1)
                    if 10 <= s < 14:
                        n1_high(g + 1, 2 * s - 20)
                        n1_high(g + 1, 2 * s - 19)

        @block.vector
        def _(dve):
            def own(sig, g, n):
                dve.wait_ge(sig.sem, sig.after(g, n))

            def split_lo(g, u, n=0):
                s, b = n % SLOTS, n % 2
                dve.wait_ge(w_hi.sem, w_hi.after(g, u + (n + 1)))
                dve.tensor_tensor(w_l[:, b], stage[:, s], w_h[:, b].bitcast(F32), ALU.subtract).then_inc(w_lo.sem, 1)

            def acc_add(N, g, k):
                dve.wait_ge(N["sq_ready"].sem, N["sq_ready"].after(g, k + 1))
                if k == 0:
                    dve.tensor_copy(acc[:], sq[:, 0]).then_inc(N["acc_ready"].sem, 1)
                else:
                    own(N["acc_ready"], g, k)
                    dve.tensor_tensor(acc[:], acc[:], sq[:, k % 2], ALU.add).then_inc(N["acc_ready"].sem, 1)

            def n1_norm(g, k):
                if k >= 2:
                    own(N1["h_ready"], g, k - 1)
                dve.scalar_tensor_tensor(out=ht[:, k % 2], in0=x_next[:, k], scalar=prm[:, C_N1 + k:C_N1 + k + 1],
                                         in1=rt[:], op0=ALU.mult, op1=ALU.mult).then_inc(ht_ready.sem, 1)

            def n1_low(g, k):
                dve.wait_ge(N1["hh_ready"].sem, N1["hh_ready"].after(g, k + 1))
                dve.tensor_tensor(h_l[:, k], ht[:, k % 2], h_h[:, k].bitcast(F32), ALU.subtract).then_inc(N1["h_ready"].sem, 1)

            dve.memset(eps[:], EPS).then_inc(init_done, 1)
            dve.memset(state[:], 0.0)
            dve.memset(tail[:], 0.0)
            dve.memset(row[:], 0.0)
            dve.memset(kn[:], 0.0)
            dve.memset(vt[:], 0.0)
            dve.wait_ge(par_loaded, 16)
            dve.tensor_scalar(nsink[:], prm[:, C_SINK:C_SINK + 8], -1.0, None, ALU.mult)
            dve.wait_ge(init_act, 1)
            dve.tensor_scalar(nalog[32:36], nalog[32:36], -1.0, None, ALU.mult).then_inc(init_done, 1)
            dve.wait_ge(init_done, 2)
            dve.sem_inc(w_lo.sem, SLOTS)
            dve.sem_inc(res.sem, 1)
            dve.sem_inc(fb_ready.sem, 2)
            dve.sem_inc(ff_ready.sem, 2)
            split_lo(0, 0)

            for k in range(KT):
                acc_add(N1, 0, k)
            dve.wait_ge(N1["rt_ready"].sem, N1["rt_ready"].after(0, 1))
            for k in range(KT + 1):
                if k < KT:
                    n1_norm(0, k)
                if k:
                    n1_low(0, k - 1)

            with dve.Fori(0, GROUPS) as g:
                split_lo(g, 0, 1)
                with dve.Fori(0, CONV // 4) as i:
                    for s in range(4):
                        m = i * 4 + s
                        dve.wait_ge(raw_ready.sem, raw_ready.after(g, m * 3 + 3))
                        dve.wait_ge(silu_done.sem, silu_done.after(g, m - 1))
                        dve.tensor_scalar(cy[:, s % 2], raw[:, s % 2, 0:TOK], convw(prm, m, 0), None,
                                          ALU.mult).then_inc(tap_done.sem, 1)
                        for j in range(1, 4):
                            own(tap_done, g, m * 4 + j)
                            dve.scalar_tensor_tensor(out=cy[:, s % 2], in0=raw[:, s % 2, j:j + TOK],
                                                     scalar=convw(prm, m, j), in1=cy[:, s % 2],
                                                     op0=ALU.mult, op1=ALU.add).then_inc(tap_done.sem, 1)
                            if j == 1:
                                split_lo(g, i * 4, s + 2)
                for m in range(1, GATE):
                    split_lo(g, CONV, m + 1)

                def src(n):
                    return qkvz[:, n, :] if n < 8 else akr[:] if n == 8 else aq[:, n - 9]

                def norm_square(n):
                    if n == 0:
                        dve.wait_ge(silu_done.sem, silu_done.after(g, 8))
                    if n >= 8:
                        dve.wait_ge(copied.sem, copied.after(g, n - 6))
                    dve.tensor_tensor(nq[:, n % 2], src(n), src(n), ALU.mult).then_inc(nsq_ready.sem, 1)

                def norm_apply(n):
                    dve.wait_ge(nrr_ready.sem, nrr_ready.after(g, n + 1))
                    dst = kn[:, HD:] if n == 8 else src(n)
                    scale = (float(P) ** -0.5 if n < 4 else 1.0 if n < 8 else
                             prm[:, C_KN:C_KN + 1] if n == 8 else prm[:, C_QN:C_QN + 1])
                    if n == 8:
                        dve.tensor_copy(kn[:, 0:HD], kn[:, TOK:]).then_inc(normed.sem, 1)
                        own(normed, g, 9)
                    dve.scalar_tensor_tensor(out=dst, in0=src(n), scalar=scale, in1=rr[:, n % 2],
                                             op0=ALU.mult, op1=ALU.mult).then_inc(normed.sem, 1)

                rd = [0]

                def row_step(ins):
                    ins.then_inc(row_dve.sem, 1)
                    rd[0] += 1
                    own(row_dve, g, rd[0])

                split_lo(g, U_BA, 1)
                norm_square(0)
                norm_square(1)
                dve.wait_ge(row_act.sem, row_act.after(g, 1))
                row_step(dve.scalar_tensor_tensor(out=rw[32:64, 1], in0=rw[32:64, 0], scalar=-1.0, in1=rw[32:64, 0],
                                                  op0=ALU.mult, op1=ALU.max))
                norm_apply(0)
                norm_square(2)
                split_lo(g, U_BA, 2)
                norm_apply(1)
                norm_square(3)
                dve.wait_ge(row_act.sem, row_act.after(g, 3))
                row_step(dve.tensor_scalar(U, E, 1.0, None, ALU.add))
                row_step(dve.scalar_tensor_tensor(out=E, in0=U, scalar=-1.0, in1=E, op0=ALU.add, op1=ALU.subtract))
                norm_apply(2)
                norm_square(4)
                split_lo(g, U_BA, 3)
                norm_apply(3)
                norm_square(5)
                norm_apply(4)
                norm_square(6)

                def softplus():
                    dve.wait_ge(row_act.sem, row_act.after(g, 5))
                    row_step(dve.tensor_copy(row[0:4], rw[0:4, 2]))
                    row_step(dve.tensor_tensor(E, E, U, ALU.mult))
                    row_step(dve.tensor_tensor(L, L, E, ALU.subtract))
                    row_step(dve.scalar_tensor_tensor(out=L, in0=X, scalar=0.0, in1=L, op0=ALU.max, op1=ALU.add))

                def cumulate():
                    row_step(dve.tensor_scalar(rw[A4, 3], rw[A4, 3], nalog[A4], None, ALU.mult))
                    for t in range(TILES):
                        tile = slice(t * P, t * P + P)
                        row_step(dve.tensor_tensor_scan(row[A4, tile], cst[A4, K_ONE, :], rw[A4, 3, tile], 0.0,
                                                        ALU.mult, ALU.add))
                    assert rd[0] == row_dve.per_group

                for j in range(PAIRS):
                    split_lo(g, U_BA, 4 + j)
                    norm_apply(5 + 2 * j)
                    norm_square(7 + 2 * j) if 7 + 2 * j < NORMS else None
                    norm_apply(6 + 2 * j) if j < 3 else None
                    norm_square(8 + 2 * j) if 8 + 2 * j < NORMS else None
                    if j == 0:
                        softplus()
                    if j == 1:
                        cumulate()
                dve.wait_ge(B1["p_rowt"].sem, B1["p_rowt"].after(g, 1))
                dve.tensor_copy(sm[:, :, 0:8].rearrange("p t (c h) -> p t c h", c=2),
                                ps[:, OV, 0:256].rearrange("p (t c h) -> p t c h", t=TILES, c=2)[:, :, :, 0:4]
                                ).then_inc(B1["tok"].sem, 1)
                own(B1["tok"], g, 1)
                dve.tensor_scalar(sm[:, :, NGC], sm[:, :, GC], -1.0, None, ALU.mult).then_inc(B1["ng"].sem, 1)

                def wt(s, t):
                    dve.wait_ge(s.sem, s.after(g, t + 1))

                def decay(t):
                    a = t % 2
                    wt(B["p_gr"], t)
                    dve.tensor_tensor(d1[:, a], heads(ring(a, 0)), per_head(cst[:, K_CAUS, :]),
                                      ALU.add).then_inc(B["dta_r"].sem, 1)
                    dve.tensor_tensor(sm[:, t, DGC].unsqueeze(2), heads(ring(a, 0))[:, :, P - 1:P],
                                      sm[:, t, GC].unsqueeze(2), ALU.subtract).then_inc(B["d2"].sem, 1)

                def inverse_input(t):
                    a = t % 2
                    wt(B["p_br"], t)
                    wt(B["dt_r"], t)
                    dve.tensor_tensor(d1[:, a], heads(ring(a, 1)), dt_[:, a], ALU.mult).then_inc(B["db_r"].sem, 1)
                    wt(B["db_r"], t)
                    wt(B["p_gg"], t)
                    dve.tensor_tensor(at_[:, a], heads(ring(a, 0)), d1[:, a], ALU.mult).then_inc(B["at_r"].sem, 1)

                def inverse_start(t):
                    a = t % 2
                    wt(B["at_r"], t)
                    if t == 0:
                        own(normed, g, NORMS + 1)
                    dve.tensor_tensor(xi[:, a], at_[:, a], per_head(cst[:, K_M0, :]), ALU.mult).then_inc(B["x0a"].sem, 1)

                decay(0)
                decay(1)
                dve.memset(pp[:, :, :, 0:HD], 0.0).then_inc(pads.sem, 1)
                inverse_input(0)
                inverse_input(1)
                norm_apply(12)
                inverse_start(0)
                inverse_start(1)
                own(B1["egt"], g, 1)
                dve.scalar_tensor_tensor(out=sm[:, :, CB], in0=sm[:, :, EGC], scalar=-1.0, in1=sm[:, :, BETA],
                                         op0=ALU.mult, op1=ALU.mult).then_inc(B1["c1"].sem, 1)

                def scores(n):
                    b, j = n % 2, n % PAIRS
                    dve.wait_ge(A["p_sc"].sem, A["p_sc"].after(g, n + 1))
                    var = (g + 3) // 4 if n < PAIRS else 1
                    if n == 0:
                        dve.wait_ge(bias_loaded, 16)
                    dve.scalar_tensor_tensor(out=ss[:, b], in0=ps[:, SC:SC + 2, 0:KEYS], scalar=HD ** -0.5,
                                             in1=bia[:, var, j], op0=ALU.mult, op1=ALU.add).then_inc(A["ss_r"].sem, 1)
                    own(A["ss_r"], g, n + 1)
                    dve.tensor_reduce(att[:, b, MAX], ss[:, b], AX.X, ALU.max).then_inc(A["amax"].sem, 1)
                    own(A["amax"], g, n + 1)
                    dve.scalar_tensor_tensor(out=att[:, b, NMAX], in0=att[:, b, MAX], scalar=-1.0,
                                             in1=nsink[:, 2 * j:2 * j + 2], op0=ALU.mult, op1=ALU.min).then_inc(A["nmax"].sem, 1)

                def softmax(n):
                    b = n % 2
                    dve.wait_ge(A["es_r"].sem, A["es_r"].after(g, n + 1))
                    dve.tensor_tensor(att[:, b, RDEN], att[:, b, SUM], att[:, b, SEXP], ALU.add).then_inc(A["den_r"].sem, 1)
                    own(A["den_r"], g, n + 1)
                    dve.reciprocal(att[:, b, RDEN], att[:, b, RDEN]).then_inc(A["rden"].sem, 1)

                def att_out(t):
                    tile = slice(t * P, t * P + P)
                    dve.wait_ge(ahi.sem, ahi.after(g, t + 1))
                    dve.tensor_tensor(h_l[:, 4:8, tile], heads(OV), h_h[:, 4:8, tile].bitcast(F32),
                                      ALU.subtract).then_inc(alo.sem, 1)

                for q in range(TILES // 2):
                    def attend(stage):
                        for k in STEPS[q].get(stage, ()):
                            if ends_tile(k) is not None and stage == "w":
                                att_out(ends_tile(k))
                            if k < TILES * PAIRS:
                                scores(k)
                            if 0 <= k - 1 < TILES * PAIRS:
                                softmax(k - 1)

                    def w(s, a):
                        wt(s, 2 * q + a)

                    def w2(s):
                        dve.wait_ge(s.sem, s.after(g, q + 1))

                    if q:
                        att_out(ends_tile(STEPS[q]["before"][0]))
                        for a in range(2):
                            decay(2 * q + a)
                    attend("before")
                    for a in range(2 if q else 0):
                        inverse_input(2 * q + a)
                        inverse_start(2 * q + a)
                    attend("gram")
                    for a in range(2):
                        w(B["p_kq"], a)
                        dve.tensor_tensor(qk[:, a], heads(ring(a, 1)), dt_[:, a], ALU.mult).then_inc(B["qk_r"].sem, 1)
                    attend("query")
                    if q == 0:
                        split_lo(g, U_BA, 8)

                    def value_rows(a):
                        t = 2 * q + a
                        w(B["p_vt"], a)
                        dve.tensor_tensor(two_by_two(qkvz[:, 8:12, t * P:t * P + P]), rows_bank(), two_by_two(wide(sm[:, t, BETA])),
                                          ALU.mult).then_inc(B["vb_r"].sem, 1)

                    def key_rows(a):
                        t = 2 * q + a
                        w(B["p_kt"], a)
                        own(B1["c1"], g, 1)
                        dve.tensor_tensor(two_by_two(kb[:, a]), rows_bank(), two_by_two(wide(sm[:, t, CB])), ALU.mult).then_inc(B["kb_r"].sem, 1)
                        w2(B2["c2"])
                        dve.tensor_tensor(two_by_two(qkvz[:, 4:8, t * P:t * P + P]), rows_bank(), two_by_two(wide(sm[:, t, CD])),
                                          ALU.mult).then_inc(B["kd_r"].sem, 1)

                    for l in range(LEVELS):
                        for a in range(2):
                            n = q * 2 * LEVELS + 2 * l + a
                            dve.wait_ge(p_y.sem, p_y.after(g, n + 1))
                            dve.tensor_tensor(flat(d1[:, a])[:, 0:256].rearrange("p (h c) -> p h c", h=HEADS),
                                              ps[:, ring(a, 3 * l + (l == 0)), 0:256].rearrange("p (h c) -> p h c", h=HEADS),
                                              cst_lev(cst, l).unsqueeze(1).to_broadcast([P, HEADS, 64]),
                                              ALU.mult).then_inc(y_ready.sem, 1)
                        if l < 4:
                            (value_rows, key_rows)[l % 2](l // 2)
                        for k in STEPS[q].get(f"level{l - 1}", ()):
                            if ends_tile(k) is not None:
                                att_out(ends_tile(k))
                        for a in range(2):
                            n = q * 2 * LEVELS + 2 * l + a
                            dve.wait_ge(p_u.sem, p_u.after(g, n + 1))
                            tc = first_half(flat(ti[:, a]), l)
                            dve.tensor_tensor(tc, ps[:, ring(a, 3 * l + 2), 0:256].rearrange("p (n b) -> p n b", b=2 << l),
                                              tc, ALU.add).then_inc(t_ready.sem, 1)
                        attend(f"level{l}")
                    attend("w")

                    def new_state(a):
                        w(B["p_su"], a)
                        for h in range(HEADS):
                            dve.scalar_tensor_tensor(out=state[:, (a + 1) % 2, h], in0=state[:, a, h],
                                                     scalar=eg[:, a, h, P - 1:P], in1=heads(ring(a, 1))[:, h],
                                                     op0=ALU.mult, op1=ALU.add).then_inc(s_ready.sem, 1)

                    def gated(a):
                        t = 2 * q + a
                        w(B["orr"], a)
                        dve.wait_ge(s_ready.sem, s_ready.after(g, (t + 1) * HEADS))
                        dve.scalar_tensor_tensor(out=eg[:, a], in0=heads(ring(a, 0)), scalar=prm[:, C_GN:C_GN + 1],
                                                 in1=dt_[:, a], op0=ALU.mult, op1=ALU.mult).then_inc(B["o1"].sem, 1)
                        w(B["o1"], a)
                        dve.tensor_tensor(eg[:, a], eg[:, a], qkvz[:, 12:16, t * P:t * P + P], ALU.mult).then_inc(B["o2"].sem, 1)

                    def mix_lo(a):
                        t = 2 * q + a
                        tile = slice(t * P, t * P + P)
                        w(B["mhi"], a)
                        dve.tensor_tensor(h_l[:, 0:4, tile], eg[:, a], h_h[:, 0:4, tile].bitcast(F32),
                                          ALU.subtract).then_inc(B["mlo"].sem, 1)

                    attend("value")
                    new_state(0)
                    gated(0)
                    new_state(1)
                    mix_lo(0)
                    gated(1)
                    mix_lo(1)

                dve.wait_ge(x_loaded.sem, x_loaded.after(g, 1))
                for m in range(KT):
                    split_lo(g, U_OUT, m + 1)
                    dve.wait_ge(unit_done.sem, unit_done.after(g, U_OUT + m + 1))
                    dve.tensor_tensor(xs[:, m], ps[:, m % 2, :], xs[:, m], ALU.add).then_inc(res.sem, 1)
                    if m:
                        acc_add(N2, g, m - 1)
                for k in range(KT):
                    dve.wait_ge(N2["hh_ready"].sem, N2["hh_ready"].after(g, k + 1))
                    dve.scalar_tensor_tensor(out=h_l[:, k], in0=xs[:, k], scalar=prm[:, C_N2 + k:C_N2 + k + 1],
                                             in1=h_h[:, k].bitcast(F32), op0=ALU.mult,
                                             op1=ALU.subtract).then_inc(N2["h_ready"].sem, 1)
                    if k == 2:
                        acc_add(N2, g, KT - 1)

                def up(half, i, s, first=False):
                    n = i * 4 + (half * 16 + s)
                    u = i * 4 + (U_MLP + 32 * half)
                    split_lo(g, u, s + 1)
                    if first:
                        dve.wait_ge(N2["rt_ready"].sem, N2["rt_ready"].after(g, 1))
                    dve.wait_ge(unit_done.sem, unit_done.after(g, u + (s + 1)))
                    dve.scalar_tensor_tensor(out=fb[:, s % 2], in0=ps[:, s % 2, :], scalar=0.0, in1=rt[:],
                                             op0=ALU.max, op1=ALU.mult).then_inc(fb_ready.sem, 1)
                    own(fb_ready, g, n + 1)
                    own(ff_ready, g, n - 1)
                    dve.tensor_tensor(ff[:, s % 2], fb[:, s % 2], fb[:, s % 2], ALU.mult).then_inc(fp_ready.sem, 1)
                    own(fp_ready, g, n + 1)
                    dve.wait_ge(fh_ready.sem, fh_ready.after(g, n + 1))
                    dve.tensor_tensor(ff_l[:, i * 4 + s, :], ff[:, s % 2], ff_h[:, i * 4 + s, :].bitcast(F32),
                                      ALU.subtract).then_inc(ff_ready.sem, 1)

                def down(half, i, s, between=()):
                    u = i * 4 + (U_MLP + 16 + 32 * half)
                    split_lo(g, u, s + 1)
                    for k in between:
                        acc_add(N1, g + 1, k)
                    if s % 2:
                        m = i * 2 + s // 2
                        dve.wait_ge(unit_done.sem, unit_done.after(g, u + (s + 1)))
                        dve.tensor_tensor(xs[:, m, :], ps[:, s // 2 % 2, :], xs[:, m, :], ALU.add).then_inc(res.sem, 1)

                for s in range(4):
                    up(0, 0, s, s == 0)
                with dve.Fori(1, 4) as i:
                    for s in range(4):
                        up(0, i, s)
                with dve.Fori(0, 4) as i:
                    for s in range(4):
                        down(0, i, s)
                with dve.Fori(0, 4) as i:
                    for s in range(4):
                        up(1, i, s)
                for s in range(16):
                    down(1, 0, s, (2 * s - 8, 2 * s - 7) if 4 <= s < 8 else ())
                    if s == 9:
                        dve.wait_ge(N1["rt_ready"].sem, N1["rt_ready"].after(g + 1, 1))
                    if 10 <= s < 14:
                        for k in (2 * s - 20, 2 * s - 19):
                            n1_norm(g + 1, k)
                        for k in (2 * s - 20, 2 * s - 19):
                            n1_low(g + 1, k)

        @block.tensor
        def _(pe):
            def mm(o, a, b, start=True, stop=True):
                return pe.matmul(o, a, b, start=start, stop=stop)

            def unit(g, u, n, bank, rhs, start=True, stop=True, first=None, order=range(KT)):
                b = n % 2
                r_h, r_l = rhs
                pe.wait_ge(w_lo.sem, w_lo.after(g, u + (n + 1)))
                o = ps[:, bank, :]
                for k in order:
                    if first:
                        first(k)
                    mm(o, w_h[:, b, k], r_h(k), start and k == order[0], False)
                    mm(o, w_h[:, b, k], r_l(k), False, False)
                    last = mm(o, w_l[:, b, k], r_h(k), False, stop and k == order[-1])
                last.then_inc(unit_done.sem, 1)

            hid = (lambda k: h_h[:, k], lambda k: h_l[:, k])

            pe.wait_ge(const_loaded, 16)
            pe.wait_ge(init_done, 2)
            pe.sem_inc(unit_done.sem, 2)

            def mean(N, g):
                pe.wait_ge(N["acc_ready"].sem, N["acc_ready"].after(g, KT))
                mm(ps[:, OV, :], cst[:, K_MEANX, :], acc[:]).then_inc(N["mean_done"].sem, 1)

            mean(N1, 0)
            with pe.Fori(0, GROUPS) as g:
                def n1_ready(k):
                    pe.wait_ge(N1["h_ready"].sem, N1["h_ready"].after(g, k + 1))

                with pe.Fori(0, CONV // 4) as i:
                    for s in range(4):
                        pe.wait_ge(raw_ready.sem, raw_ready.after(g, (i * 4 + s) * 3 - 3))
                        unit(g, i * 4, s, A0 + s % 2, hid, first=n1_ready if s == 0 else None)
                for m in range(GATE):
                    if m < 2:
                        pe.wait_ge(raw_ready.sem, raw_ready.after(g, (CONV + m) * 3 - 3))
                    else:
                        pe.wait_ge(z_ready.sem, z_ready.after(g, m - 1))
                    unit(g, CONV, m, A0 + m % 2, hid)

                def norm_sum(n):
                    pe.wait_ge(nsq_ready.sem, nsq_ready.after(g, n + 1))
                    mm(ps[:, NS + (n + 1) % 2, :], cst[:, K_ONE if n < 8 else K_HALF, :], nq[:, n % 2]).then_inc(nsum_done.sem, 1)

                pe.wait_ge(z_ready.sem, z_ready.after(g, 3))
                unit(g, U_BA, 0, A0, hid)
                norm_sum(0)
                pe.wait_ge(z_ready.sem, z_ready.after(g, 4))
                unit(g, U_BA, 1, A0 + 1, hid)
                norm_sum(1)
                norm_sum(2)
                pe.wait_ge(row_act.sem, row_act.after(g, 2))
                unit(g, U_BA, 2, A0, hid)
                norm_sum(3)
                norm_sum(4)
                pe.wait_ge(copied.sem, copied.after(g, 1))
                for t in range(TILES):
                    last = pe.transpose(heads(OV)[:, t], avr[:, t * P:t * P + P], I)
                last.then_inc(vt_sum.sem, 1)
                def wt(s, t):
                    pe.wait_ge(s.sem, s.after(g, t + 1))

                def four(o, f, sig):
                    for h in range(HEADS):
                        last = f(o[:, h], h)
                    last.then_inc(sig.sem, 1)

                def decay(t):
                    a, tile = t % 2, row[0:64, t * P:t * P + P]
                    four(heads(ring(a, 0)), lambda o, h: mm(o, cst[0:64, K_SEL + 4 + h, :], tile), B["p_gr"])
                    four(heads(ring(a, 1)), lambda o, h: mm(o, cst[0:64, K_SEL + h, :], tile), B["p_br"])

                for j in range(PAIRS):
                    pe.wait_ge(copied.sem, copied.after(g, j + 1))
                    unit(g, U_BA, 3 + j, A0 + (U_AQ + j) % 2, hid)
                    norm_sum(5 + 2 * j)
                    if j == PAIRS - 1:
                        pe.wait_ge(row_dve.sem, row_dve.after(g, row_dve.per_group))
                        pe.nop(nofuse=True)
                        for t in range(TILES):
                            last = pe.transpose(ps[:, OV, 64 * t:64 * t + 64], row[0:64, t * P:(t + 1) * P],
                                                cst[0:64, K_ID, 0:64])
                        last.then_inc(B1["p_rowt"].sem, 1)
                        decay(0)
                        pe.wait_ge(copied.sem, copied.after(g, 6))
                        decay(1)
                    norm_sum(6 + 2 * j)

                def sc(n):
                    t, j = n // PAIRS, n % PAIRS
                    if n:
                        pe.wait_ge(A["ss_r"].sem, A["ss_r"].after(g, n))
                    if n < PAIRS:
                        pe.wait_ge(normed.sem, normed.after(g, NORMS + n // (PAIRS - 1)))
                    for e in range(2):
                        r = slice(HD * e, HD * e + HD)
                        last = mm(ps[:, SC + e, 0:KEYS], aq[r, j, t * P:t * P + P], kn[r, t * P:t * P + KEYS])
                    last.then_inc(A["p_sc"].sem, 1)

                def pt(n):
                    pe.wait_ge(A["p_ready"].sem, A["p_ready"].after(g, n + 1))
                    o = ps[:, PT, :].rearrange("p (e c k) -> p e c k", e=2, c=2)
                    for e in range(2):
                        for c in range(2):
                            last = pe.transpose(o[:, e, c], pp[:, n % 2, e, c * P:c * P + P], I)
                    last.then_inc(A["p_pt"].sem, 1)

                def ov(n):
                    t, j = n // PAIRS, n % PAIRS
                    pe.wait_ge(A["ptc"].sem, A["ptc"].after(g, n + 1))
                    if n == 0:
                        pe.wait_ge(vt_ready.sem, vt_ready.after(g, 2))
                    if t and j == 0:
                        pe.wait_ge(alo.sem, alo.after(g, t))
                    for e in range(2):
                        r = slice(HD * e, HD * e + HD)
                        for c in range(2):
                            last = mm(heads(OV)[r, j], vt[:, t + c, r], pts[:, n % 2, e, c], c == 0, c == 1)
                    if j == PAIRS - 1:
                        last.then_inc(p_ov.sem, 1)

                for q in range(TILES // 2):
                    def attend(stage):
                        for k in STEPS[q].get(stage, ()):
                            if k < TILES * PAIRS:
                                sc(k)
                            if 0 <= k - 3 < TILES * PAIRS:
                                ov(k - 3)
                            if stage == "before":
                                w(B["oln"], -1)
                            if 0 <= k - 2 < TILES * PAIRS:
                                pt(k - 2)

                    def w(s, a):
                        wt(s, 2 * q + a)

                    def part(i, a):
                        return qkvz[:, 4 * i:4 * i + 4, (2 * q + a) * P:(2 * q + a + 1) * P]

                    attend("before")
                    for a in range(2 if q else 0):
                        w(B["o1"], a - 2)
                        decay(2 * q + a)
                    for a in range(2):
                        w(B["eg_r"], a)
                        four(heads(ring(a, 0)), lambda o, h: mm(o, part(1, a)[:, h], part(1, a)[:, h]), B["p_gg"])
                    attend("gram")
                    for a in range(2):
                        w(B["db_r"], a)
                        four(heads(ring(a, 1)), lambda o, h: mm(o, part(1, a)[:, h], part(0, a)[:, h]), B["p_kq"])
                    attend("query")
                    for a in range(2):
                        w(B["x0"], a)
                        four(heads(ring(a, 0)), lambda o, h: pe.transpose(o, xi[:, a, h], I), B["p_t0"])

                    def token_rows(l):
                        a, i, sig = l // 2, (2, 1)[l % 2], (B["p_vt"], B["p_kt"])[l % 2]
                        if l:
                            w(B["kd_r"], a - 1) if l % 2 == 0 else w(B["vb_r"], a)
                        n = STEPS[q][f"level{l - 1}" if f"level{l - 1}" in STEPS[q] else "query"][0] + 1
                        pe.wait_ge(A["ss_r"].sem, A["ss_r"].after(g, n))
                        for h in range(HEADS):
                            last = pe.transpose(rows_bank()[:, h // 2, h % 2], part(i, a)[:, h], I)
                        last.then_inc(sig.sem, 1)

                    def rows_out(l):
                        w((B["vb_r"], B["kd_r"])[l % 2], l // 2)

                    for l in range(LEVELS + 1):
                        n = q * 2 * LEVELS + 2 * l
                        for a in range(2 if l < LEVELS else 0):
                            if l == 0:
                                w(B["t0"], a)
                                w(B["qk_r"], a)
                            else:
                                pe.wait_ge(t_ready.sem, t_ready.after(g, n - 2 + a + 1))
                            o = ps[:, ring(a, 3 * l + (l == 0)), 0:256].rearrange("p (h n b) -> p h n b", h=HEADS, b=2 << l)
                            four(o, lambda o, h: mm(o, at_[:, a, h], first_half(ti[:, a, h], l)), p_y)
                        for a in range(2 if l else 0):
                            pe.wait_ge(t_ready.sem, t_ready.after(g, n - 2 + a + 1))
                            four(heads(ring(a, 3 * l + 1)), lambda o, h: pe.transpose(o, ti[:, a, h], I), p_x)
                        if l < 4:
                            token_rows(l)
                        for a in range(2 if l < LEVELS else 0):
                            if l:
                                pe.wait_ge(x_ready.sem, x_ready.after(g, n - 2 + a + 1))
                            pe.wait_ge(y_ready.sem, y_ready.after(g, n + a + 1))
                            o = ps[:, ring(a, 3 * l + 2), 0:256].rearrange("p (h c) -> p h c", h=HEADS)
                            four(o, lambda o, h: mm(o, xi[:, a, h], flat(d1[:, a])[:, 64 * h:64 * h + 64]), p_u)
                        if l < 4:
                            rows_out(l)
                        attend(f"level{l}")
                    for a in range(2):
                        pe.wait_ge(x_ready.sem, x_ready.after(g, (q + 1) * 2 * LEVELS - 1 + a))
                        four(heads(ring(a, 0)), lambda o, h: mm(o, kb[:, a, h], xi[:, a, h]), B["p_wt"])

                    def values(a):
                        w(B["wtc"], a)
                        if 2 * q + a:
                            pe.wait_ge(s_ready.sem, s_ready.after(g, (2 * q + a) * HEADS))
                        o = heads(ring(a, 1))
                        for h in range(HEADS):
                            mm(o[:, h], xi[:, a, h], part(2, a)[:, h], True, False)
                            last = mm(o[:, h], ti[:, a, h], state[:, a, h], False, True)
                        last.then_inc(B["p_vv"].sem, 1)

                    def state_and_out(a):
                        w(B["vnc"], a)
                        four(heads(ring(a, 1)), lambda o, h: mm(o, part(1, a)[:, h], d1[:, a, h]), B["p_su"])
                        w(B["qd_r"], a)
                        o = heads(ring(a, 0))
                        for h in range(HEADS):
                            mm(o[:, h], state[:, a, h], part(0, a)[:, h], True, False)
                            last = mm(o[:, h], d1[:, a, h], qk[:, a, h], False, True)
                        last.then_inc(B["p_oo"].sem, 1)

                    def out_mean(a):
                        w(B["osq_r"], a)
                        if a:
                            w(B["oln"], 0)
                        elif q == 0:
                            pe.wait_ge(A["ptc"].sem, A["ptc"].after(g, STEPS[q]["value"][0] - 1))
                        mm(ps[:, PT, :], cst[:, K_MEAN, :], flat(at_[:, a])).then_inc(B["p_on"].sem, 1)

                    attend("w")
                    values(0)
                    attend("value")
                    state_and_out(0)
                    values(1)
                    out_mean(0)
                    state_and_out(1)
                    out_mean(1)

                last = pe.transpose(ps[:, SC, 0:P], I, I)
                last.then_inc(unit_done.sem, 1)
                def mix_ready(k):
                    if k == HEADS:
                        pe.wait_ge(alo.sem, alo.after(g, TILES))
                    if k == 0:
                        pe.wait_ge(B["mlo"].sem, B["mlo"].after(g, TILES))

                for m in range(KT):
                    if m >= 2:
                        pe.wait_ge(res.sem, res.after(g, m - 1))
                    unit(g, U_OUT, m, m % 2, hid, first=mix_ready if m == 0 else None,
                         order=(4, 5, 6, 7, 0, 1, 2, 3))

                def up(half, i, s):
                    pe.wait_ge(fb_ready.sem, fb_ready.after(g, i * 4 + (16 * half + s - 1)))
                    if half and s == 1:
                        pe.wait_ge(res.sem, res.after(g, 2 * KT))
                    unit(g, i * 4 + (U_MLP + 32 * half), s, s % 2, hid)

                def down(half, i, s):
                    kq = s % 2
                    if s == 2:
                        pe.wait_ge(fb_ready.sem, fb_ready.after(g, 16 * half + 16))
                    if kq == 0:
                        pe.wait_ge(res.sem, res.after(g, i * 2 + (KT + KT * half + s // 2 - 1)))
                    pe.wait_ge(ff_ready.sem, ff_ready.after(g, 16 * half + 8 * kq + 8))
                    hidden = (lambda k: ff_h[:, 8 * kq + k], lambda k: ff_l[:, 8 * kq + k])
                    unit(g, i * 4 + (U_MLP + 16 + 32 * half), s, s // 2 % 2, hidden, kq == 0, kq == 1)

                def next_ready(k):
                    pe.wait_ge(N2["h_ready"].sem, N2["h_ready"].after(g, k + 1))

                pe.wait_ge(res.sem, res.after(g, KT - 1))
                for s in range(4):
                    if s == 0:
                        unit(g, U_MLP, 0, 0, hid, first=next_ready)
                        mean(N2, g)
                    else:
                        if s == 1:
                            pe.wait_ge(res.sem, res.after(g, KT))
                        up(0, 0, s)
                with pe.Fori(1, 4) as i:
                    for s in range(4):
                        up(0, i, s)
                for half in range(2):
                    if half:
                        pe.wait_ge(res.sem, res.after(g, 2 * KT - 1))
                        pe.nop(nofuse=True)
                        with pe.Fori(0, 4) as i:
                            for s in range(4):
                                up(1, i, s)
                    pe.wait_ge(fb_ready.sem, fb_ready.after(g, 16 * half + 15))
                    pe.nop(nofuse=True)
                    for quarter in range(2):
                        with pe.Fori(2 * quarter, 2 * quarter + 2) as i:
                            for s in range(4):
                                down(half, i, s)
                        if half and quarter == 0:
                            mean(N1, g + 1)


def cst_lev(cst, l):
    return cst[:, K_LEV:K_LEV + 3, :].rearrange("p n c -> p (n c)")[:, 64 * l:64 * l + 64]


def convw(prm, m, j):
    return prm[:, C_CONV:C_CONV + 4 * CONV].rearrange("p (m j) -> p m j", j=4)[:, m, j:j + 1]


def u_div(u, n):
    return u // SLOTS + n // SLOTS



def constants():
    i = np.arange(P)
    c = np.zeros((P, N_CONST, P), np.float32)
    c[:, K_ID] = np.eye(P)
    c[:, K_ONE] = 1.0
    c[:, K_MEAN] = 1.0 / P
    c[:, K_MEANX] = 1.0 / D
    c[:, K_HALF] = (i[:, None] // HD == i[None, :] // HD) / HD
    c[:, K_CAUS] = np.where(i[:, None] <= i[None, :], 0.0, NEG)
    c[:, K_M0] = -1.0 * ((i[:, None] % 2 == 0) & (i[None, :] == i[:, None] + 1))
    for l in range(LEVELS):
        b = 2 << l
        j = i[i % (2 * b) < b]
        c[:, K_LEV + l // 2, 64 * (l % 2):64 * (l % 2) + 64] = -1.0 * (
            (i[:, None] // (2 * b) == j[None, :] // (2 * b)) & (i[:, None] % (2 * b) >= b))
    for h in range(HEADS):
        c[h, K_SEL + h] = 1.0
        c[32 + h, K_SEL + 4 + h] = 1.0
    q, k = i[:, None], np.arange(KEYS)[None, :]
    dist = np.abs(q + HD - k).astype(np.float32)
    seen = np.where(q < HD, k < 2 * HD, k >= HD)
    b = np.zeros((P, 2, PAIRS, 2, KEYS), np.float32)
    for j in range(PAIRS):
        for e in range(2):
            slope = np.float32(2.0 ** -(4 * e + j + 1))
            b[:, 0, j, e] = np.where(seen & (k >= HD), -slope * dist, NEG)
            b[:, 1, j, e] = np.where(seen, -slope * dist, NEG)
    return c.reshape(P, -1), b.reshape(P, -1)


def weight_units(w_in, w_out, w1, w2):
    def tile(m):
        return m.reshape(KT, P, P).transpose(1, 0, 2).reshape(P, KT * P)

    u = np.zeros((UNITS, P, KT * P), np.float32)
    for m in range(16):
        u[m] = tile(w_in[:, m * P:m * P + P])
    ba = np.zeros((D, P), np.float32)
    ba[:, 0:4] = w_in[:, 2048:2052]
    ba[:, 32:36] = w_in[:, 2052:2056]
    u[U_BA] = tile(ba)
    q0, k0, v0 = 2056, 2568, 2696
    for j in range(PAIRS):
        cols = [q0 + HD * h + c for h in (j, 4 + j) for c in range(HD)]
        u[U_AQ + j] = tile(w_in[:, cols])
    u[U_AK] = tile(w_in[:, k0:k0 + P])
    u[U_AV] = tile(w_in[:, v0:v0 + P])
    rows = list(range(512)) + [512 + HD * h + c for j in range(PAIRS) for h in (j, 4 + j) for c in range(HD)]
    wo = w_out[rows]
    for m in range(KT):
        cols = slice(m * P, m * P + P)
        u[U_OUT + m] = tile(wo[:, cols])
        for half in range(2):
            for kq in range(2):
                r = half * 2048 + kq * 1024
                u[U_MLP + 16 + 32 * half + 2 * m + kq] = tile(w2[r:r + 1024, cols])
    for m in range(32):
        u[U_MLP + 32 * (m // 16) + m % 16] = tile(w1[:, m * P:m * P + P])
    return u


def parameters(norm1_w, norm2_w, conv_w, gdn_norm_w, q_norm_w, k_norm_w, a_log, dt_bias, sinks):
    p = np.zeros((P, N_PAR), np.float32)
    p[:, C_N1:C_N1 + 8] = norm1_w[0].reshape(8, P).T
    p[:, C_N2:C_N2 + 8] = norm2_w[0].reshape(8, P).T
    p[:, C_CONV:C_CONV + 48] = conv_w[0].reshape(4, CONV, P).transpose(2, 1, 0).reshape(P, 48)
    p[:, C_GN] = gdn_norm_w[0]
    p[:, C_QN] = np.concatenate([q_norm_w[0]] * 2)
    p[:, C_KN] = np.concatenate([k_norm_w[0]] * 2)
    p[32:36, C_ALOG] = a_log[0]
    p[32:36, C_DT] = dt_bias[0]
    p[:, C_SINK:] = sinks[0].reshape(2, PAIRS).T.reshape(-1)[None, :]
    return p


def kernel(x, norm1_w, w_in, conv_w, a_log, dt_bias, gdn_norm_w, q_norm_w, k_norm_w, sinks, w_out, norm2_w, w1, w2):
    import concourse.bacc as bacc
    from concourse.bass_utils import run_bass_kernel_spmd

    (x, norm1_w, w_in, conv_w, a_log, dt_bias, gdn_norm_w, q_norm_w, k_norm_w, sinks, w_out, norm2_w, w1, w2) = (
        np.asarray(a) for a in (x, norm1_w, w_in, conv_w, a_log, dt_bias, gdn_norm_w, q_norm_w, k_norm_w, sinks,
                                w_out, norm2_w, w1, w2))
    con, bias = constants()
    arrays = {
        "x": np.ascontiguousarray(x[0].reshape(GROUPS, TOK, KT, P).transpose(0, 3, 2, 1)),
        "w": weight_units(w_in[0], w_out[0], w1[0], w2[0]),
        "par": parameters(norm1_w, norm2_w, conv_w, gdn_norm_w, q_norm_w, k_norm_w, a_log, dt_bias, sinks),
        "con": con.reshape(P, N_CONST, P),
        "bias": bias,
    }
    nc = bacc.Bacc("TRN2", target_bir_lowering=False, num_devices=1)
    ins = [nc.dram_tensor(n, a.shape, F32, kind="ExternalInput").ap() for n, a in arrays.items()]
    out = nc.dram_tensor("out", (GROUPS, P, KT, TOK), F32, kind="ExternalOutput").ap()
    build(nc, *ins, out)
    y = run_bass_kernel_spmd(nc, [arrays], core_ids=[0]).results[0]["out"]
    return np.ascontiguousarray(y.transpose(0, 3, 2, 1)).reshape(1, SEQ, D)
```
